# Optimizing a Trainium2 kernel written in Bass

```python
import jax, jax.numpy as jnp
from jax import lax
import numpy as np

D_MODEL = 2048
BATCH = 1
SEQ = 512
DEPTH = 1

CHUNK = 64
HEAD_DIM = 128
SWA_Q_HEADS = 8
SWA_KV_HEADS = 2
SWA_GROUP = SWA_Q_HEADS // SWA_KV_HEADS
WINDOW = 128
WINDOW_CHUNKS = WINDOW // CHUNK
FOX_HEADS = 8
Q_BLOCK = 128
ROPE_THETA = 10000.0
D_FF = ((8 * D_MODEL // 3 + 255) // 256) * 256
EPS = 1e-6
NEG_INF = -1e30

SWA_Q_W = SWA_Q_HEADS * HEAD_DIM
SWA_KV_W = SWA_KV_HEADS * HEAD_DIM
FOX_W = FOX_HEADS * HEAD_DIM
IN_WIDTHS = (SWA_Q_W, SWA_KV_W, SWA_KV_W, FOX_W, FOX_W, FOX_W, FOX_HEADS, D_MODEL, D_MODEL)
IN_TOTAL = sum(IN_WIDTHS)

kernel_name = 'hybrid_swa_sink_fox_swiglu_adaln_block'

def rms_norm(x, w):
    xf = x.astype(jnp.float32)
    y = xf * lax.rsqrt(jnp.mean(xf * xf, axis=-1, keepdims=True) + EPS)
    return (y * w.astype(jnp.float32)).astype(x.dtype)

def split_cols(t, widths):
    idx, acc = [], 0
    for w in widths[:-1]:
        acc += w
        idx.append(acc)
    return jnp.split(t, idx, axis=-1)

def rope(x):
    S = x.shape[1]
    half = HEAD_DIM // 2
    inv_freq = ROPE_THETA ** (-jnp.arange(half, dtype=jnp.float32) / half)
    ang = jnp.arange(S, dtype=jnp.float32)[:, None] * inv_freq[None, :]
    cos = jnp.cos(ang)[None, :, None, :]
    sin = jnp.sin(ang)[None, :, None, :]
    xf = x.astype(jnp.float32)
    x1, x2 = xf[..., :half], xf[..., half:]
    out = jnp.concatenate([x1 * cos - x2 * sin, x2 * cos + x1 * sin], axis=-1)
    return out.astype(x.dtype)

def swa_sink_attention(q, k, v, sinks):
    B, S = q.shape[0], q.shape[1]
    NC = S // CHUNK
    P = (WINDOW_CHUNKS - 1) * CHUNK
    qc = q.reshape(B, NC, CHUNK, SWA_KV_HEADS, SWA_GROUP, HEAD_DIM)

    def band(t):
        tp = jnp.pad(t, ((0, 0), (P, 0), (0, 0), (0, 0)))
        tc = tp.reshape(B, NC + WINDOW_CHUNKS - 1, CHUNK, SWA_KV_HEADS, HEAD_DIM)
        return jnp.concatenate([tc[:, i:i + NC] for i in range(WINDOW_CHUNKS)], axis=2)

    kb, vb = band(k), band(v)
    scores = jnp.einsum('bncegd,bnked->bnegck', qc, kb).astype(jnp.float32) * (HEAD_DIM ** -0.5)
    key_pos = jnp.arange(NC)[:, None] * CHUNK - P + jnp.arange(WINDOW_CHUNKS * CHUNK)[None, :]
    valid = key_pos >= 0
    scores = jnp.where(valid[None, :, None, None, None, :], scores, NEG_INF)
    sink = sinks.astype(jnp.float32).reshape(1, 1, SWA_KV_HEADS, SWA_GROUP, 1, 1)
    sink = jnp.broadcast_to(sink, scores.shape[:-1] + (1,))
    probs = jax.nn.softmax(jnp.concatenate([scores, sink], axis=-1), axis=-1)[..., :-1]
    out = jnp.einsum('bnegck,bnked->bncegd', probs.astype(v.dtype), vb)
    return out.reshape(B, S, SWA_Q_W)

def forgetting_attention(q, k, v, log_f):
    B, S = q.shape[0], q.shape[1]
    NB = S // Q_BLOCK
    Ft = jnp.cumsum(log_f, axis=1).transpose(0, 2, 1)
    qb = q.reshape(B, NB, Q_BLOCK, FOX_HEADS, HEAD_DIM).transpose(1, 0, 2, 3, 4)
    Fq = Ft.reshape(B, FOX_HEADS, NB, Q_BLOCK).transpose(2, 0, 1, 3)
    key_idx = jnp.arange(S)
    scale = HEAD_DIM ** -0.5

    def block(args):
        qi, Fi, i = args
        s = jnp.einsum('bqhd,bkhd->bhqk', qi, k).astype(jnp.float32) * scale
        s = s + Fi[..., None] - Ft[:, :, None, :]
        q_idx = i * Q_BLOCK + jnp.arange(Q_BLOCK)
        mask = key_idx[None, :] <= q_idx[:, None]
        s = jnp.where(mask[None, None], s, NEG_INF)
        p = jax.nn.softmax(s, axis=-1)
        return jnp.einsum('bhqk,bkhd->bqhd', p.astype(v.dtype), v)

    out = lax.map(block, (qb, Fq, jnp.arange(NB)))
    return out.transpose(1, 0, 2, 3, 4).reshape(B, S, FOX_W)

def setup_inputs(seed: int = 0) -> dict:
    key = jax.random.key(seed)
    ks = jax.random.split(key, 20)
    L, D = DEPTH, D_MODEL

    def nrm(k, shape, scale):
        return jax.random.normal(k, shape, jnp.float32) * scale

    return {
        'x': nrm(ks[0], (BATCH, SEQ, D), 1.0),
        'c': nrm(ks[1], (BATCH, D), 1.0),
        'w_ada': nrm(ks[2], (L, D, 6 * D), 0.5 * D ** -0.5),
        'b_ada': nrm(ks[3], (L, 6 * D), 0.01),
        'norm1_w': 1.0 + nrm(ks[4], (L, D), 0.02),
        'w_in': nrm(ks[5], (L, D, IN_TOTAL), D ** -0.5),
        'b_forget': 1.0 + nrm(ks[6], (L, FOX_HEADS), 0.5),
        'swa_q_norm_w': 1.0 + nrm(ks[7], (L, HEAD_DIM), 0.02),
        'swa_k_norm_w': 1.0 + nrm(ks[8], (L, HEAD_DIM), 0.02),
        'swa_sinks': nrm(ks[9], (L, SWA_Q_HEADS), 0.5),
        'fox_q_norm_w': 1.0 + nrm(ks[10], (L, HEAD_DIM), 0.02),
        'fox_k_norm_w': 1.0 + nrm(ks[11], (L, HEAD_DIM), 0.02),
        'w_o_swa': nrm(ks[12], (L, SWA_Q_W, D), SWA_Q_W ** -0.5),
        'w_o_fox': nrm(ks[13], (L, FOX_W, D), FOX_W ** -0.5),
        'w_out': nrm(ks[14], (L, D, D), D ** -0.5),
        'norm2_w': 1.0 + nrm(ks[15], (L, D), 0.02),
        'w_ffn_in': nrm(ks[16], (L, D, 2 * D_FF), D ** -0.5),
        'w_ffn_out': nrm(ks[17], (L, D_FF, D), D_FF ** -0.5),
    }

def reference(x, c, w_ada, b_ada, norm1_w, w_in, b_forget, swa_q_norm_w, swa_k_norm_w,
              swa_sinks, fox_q_norm_w, fox_k_norm_w, w_o_swa, w_o_fox, w_out, norm2_w,
              w_ffn_in, w_ffn_out):
    B, S = x.shape[0], x.shape[1]
    c_act = jax.nn.silu(c)
    for l in range(DEPTH):
        mod = c_act @ w_ada[l] + b_ada[l]
        shift1, scale1, gate1, shift2, scale2, gate2 = [m[:, None, :] for m in jnp.split(mod, 6, axis=-1)]

        h = rms_norm(x, norm1_w[l]) * (1.0 + scale1) + shift1
        proj = h @ w_in[l]
        q_a, k_a, v_a, q_f, k_f, v_f, f_logit, g_a, g_f = split_cols(proj, IN_WIDTHS)

        q_a = rope(rms_norm(q_a.reshape(B, S, SWA_Q_HEADS, HEAD_DIM), swa_q_norm_w[l]))
        k_a = rope(rms_norm(k_a.reshape(B, S, SWA_KV_HEADS, HEAD_DIM), swa_k_norm_w[l]))
        v_a = v_a.reshape(B, S, SWA_KV_HEADS, HEAD_DIM)
        y_a = swa_sink_attention(q_a, k_a, v_a, swa_sinks[l]) @ w_o_swa[l]

        q_f = rms_norm(q_f.reshape(B, S, FOX_HEADS, HEAD_DIM), fox_q_norm_w[l])
        k_f = rms_norm(k_f.reshape(B, S, FOX_HEADS, HEAD_DIM), fox_k_norm_w[l])
        v_f = v_f.reshape(B, S, FOX_HEADS, HEAD_DIM)
        log_f = jax.nn.log_sigmoid(f_logit.astype(jnp.float32) + b_forget[l].astype(jnp.float32))
        y_f = forgetting_attention(q_f, k_f, v_f, log_f) @ w_o_fox[l]

        merged = jax.nn.sigmoid(g_a) * y_a + jax.nn.sigmoid(g_f) * y_f
        x = x + gate1 * (merged @ w_out[l])

        h2 = rms_norm(x, norm2_w[l]) * (1.0 + scale2) + shift2
        g, u = jnp.split(h2 @ w_ffn_in[l], 2, axis=-1)
        x = x + gate2 * ((jax.nn.silu(g) * u) @ w_ffn_out[l])
    return x


_drawn_inputs = setup_inputs


def setup_inputs(seed=0):
    import zlib

    import numpy as np

    out = dict(_drawn_inputs(seed))
    spreads = {}
    factors = {'b_ada': 5.848,
     'norm1_w': 8.0,
     'swa_q_norm_w': 8.0,
     'swa_k_norm_w': 8.0,
     'swa_sinks': 8.0,
     'fox_q_norm_w': 8.0,
     'fox_k_norm_w': 8.0,
     'norm2_w': 8.0}
    for name, (base, spread) in spreads.items():
        noise = np.random.default_rng([zlib.crc32(name.encode()), seed]).standard_normal(out[name].shape)
        drawn = base * np.exp(spread * noise) if base else spread * noise
        out[name] = __import__('jax').numpy.asarray(drawn.astype(out[name].dtype))
    for name, factor in factors.items():
        out[name] = (out[name] * factor).astype(out[name].dtype)
    return out
```

```python
from contextlib import ExitStack

import numpy as np

import concourse.bass as bass
from concourse import mybir

P = 128
ALU = mybir.AluOpType
ACT = mybir.ActivationFunctionType
F32 = mybir.dt.float32
F32R = mybir.dt.float32r

D = 2048
S = 512
TB = S // P
KD = D // P
DH = 128
HQ = 8
KVH = 2
GROUP = HQ // KVH
CHUNK = 64
DFF = ((8 * D // 3 + 255) // 256) * 256
EPS = 1e-6
NEG = -1e30
SCALE = DH ** -0.5

QA0 = 0
KA0 = HQ * DH
VA0 = KA0 + KVH * DH
QF0 = VA0 + KVH * DH
KF0 = QF0 + HQ * DH
VF0 = KF0 + HQ * DH
FL0 = VF0 + HQ * DH
G0 = FL0 + HQ
IN_TOTAL = G0 + 2 * D

UK = 4
UN = 2 * P
RING = 4
LEAD = 3

F_R, Y0_R, Y1_R = 0, 4, 8
A_R, A_N, A_I = 12, 8, HQ
B_R, B_N, B_I = A_R + A_N * A_I, 8, HQ
C_R, C_N, C_I = B_R + B_N * B_I, 4, D // UN
D_R, D_N, D_I = C_R + C_N * C_I, 8, D // UN // 2
E_R, E_N, E_I = D_R + D_N * D_I, 24, DFF // (UK * P)
STEP = KD // UK
ADA0_STEPS = 2 * D // UN
ADA_A, ADA_C = ADA0_STEPS, ADA0_STEPS + 2 * A_I
ADA_D = ADA_C + C_I
F_U = STEP * ADA0_STEPS
Y0_U, Y1_U = F_U + 4, F_U + 8
A_U = F_U + 12
B_U = A_U + 2 * A_N * A_I
C_U = B_U + B_N * B_I
D_U = C_U + 2 * C_N * C_I
E_U = D_U + 2 * D_N * D_I

CONST_W = P + 3 * S + 2 * P + HQ


def shape_constants():
    half = DH // 2
    inv = (np.float32(10000.0) ** (-np.arange(half, dtype=np.float32) / np.float32(half))).astype(np.float32)
    ang = (np.arange(S, dtype=np.float32)[:, None] * inv[None, :]).astype(np.float32)
    cos, sin = np.cos(ang).T.astype(np.float32), np.sin(ang).T.astype(np.float32)
    p = np.arange(P)[:, None]
    fox = np.where((np.arange(S)[None, :] - (S - P)) <= p, 0.0, NEG)
    j = np.arange(2 * P)[None, :]
    chunk_q, chunk_k = p // CHUNK + P // CHUNK, j // CHUNK
    swa = np.where((chunk_k == chunk_q) | (chunk_k == chunk_q - 1), 0.0, NEG)
    sel = (p % 32 == np.arange(HQ)[None, :]) * 1.0
    parts = [np.eye(P), np.concatenate([cos, cos]), np.concatenate([sin, -sin]), fox, swa, sel]
    return np.ascontiguousarray(np.concatenate(parts, axis=1).astype(np.float32))


def build_block(nc, x, c, w_ada, b_ada, norm1_w, w_in, b_forget, swa_q_norm_w, swa_k_norm_w,
                swa_sinks, fox_q_norm_w, fox_k_norm_w, w_o_swa, w_o_fox, w_out, norm2_w,
                w_ffn_in, w_ffn_out, consts, out):
    with ExitStack() as ctx:
        def sem(name):
            return ctx.enter_context(nc.semaphore(name))

        T = 4 * S
        arena_base = (nc.sbuf_base + 31) // 32 * 32
        arena_bytes = nc.sbuf_usable_end - arena_base

        def at(name, offset, cols, dt=F32):
            assert offset + 4 * cols <= arena_bytes, (name, offset, cols)
            return nc.alloc_sbuf_tensor_at(name, [P, cols], dt, offset=arena_base + offset)

        H = 0
        STORE = H + 2 * KD * T
        RAW = STORE + 36 * T
        WHI = RAW + RING * 4 * UK * UN
        WLO = WHI + RING * 4 * UK * UN
        SMALL = WLO + RING * 4 * UK * UN
        FORGET = SMALL + 2560
        TAB = FORGET + 2 * T
        WORK = TAB + 2 * T

        h_hi = at("h_hi", H, KD * S, F32R)
        h_lo = at("h_lo", H + KD * T, KD * S, F32R)
        out_rows = at("out_rows", H, TB * D)
        w_raw = at("w_raw", RAW, RING * UK * UN)
        w_hi = at("w_hi", WHI, RING * UK * UN, F32R)
        w_lo = at("w_lo", WLO, RING * UK * UN, F32R)

        x_rows = at("x_rows", STORE, TB * D)
        xn = at("xn", STORE + TB * 4 * D, KD * S)
        junk = at("junk", STORE + 2 * TB * 4 * D, D)
        qf = at("qf", STORE, 8 * S)
        kf = at("kf", STORE + 8 * T, 8 * S)
        rot = at("rot", STORE + 16 * T, 10 * S)
        val = at("val", STORE + 26 * T, 10 * S)
        of_hi = at("of_hi", STORE, 8 * S, F32R)
        of_lo = at("of_lo", STORE + 8 * T, 8 * S, F32R)
        oa_hi = at("oa_hi", STORE + 18 * T, 8 * S, F32R)
        oa_lo = at("oa_lo", STORE + 28 * T, 8 * S, F32R)
        x2 = at("x2", STORE, KD * S)
        u_hi = at("u_hi", STORE + 16 * T, UK * S, F32R)
        u_lo = at("u_lo", STORE + 20 * T, UK * S, F32R)
        sg = at("sg", STORE + 24 * T, 2 * S)
        u_full = at("u_full", STORE + 26 * T, 2 * S)
        h2_t = at("h2_t", STORE + 28 * T, 2 * S)
        h2_full = at("h2_full", STORE + 30 * T, 2 * S)
        r2 = at("r2", STORE + 32 * T, S)
        xr = at("xr", STORE + 24 * T, 4 * S)
        sq2 = at("sq2", STORE + 28 * T, 2 * S)
        sumsq = at("sumsq", STORE + 30 * T, S)

        small_all = at("small_all", SMALL, (FORGET - SMALL) // 4)
        small, o = {}, 0
        for name, cols in (("ident", P), ("ones", P), ("mod", 6 * KD), ("bada", 6 * KD), ("vec", 64),
                           ("cact", KD), ("a1", KD), ("a2", KD), ("wy", 10), ("wx", 2), ("sinks", HQ),
                           ("sel", HQ), ("bf", 1), ("eps", 1), ("ss", TB), ("rr", TB), ("colraw", 2),
                           ("rowmax", TB), ("negmax", TB), ("rowsum", TB), ("esink", TB), ("rinv", TB),
                           ("sinkcol", 1)):
            small[name] = small_all[:, o:o + cols]
            o += cols
        assert SMALL + 4 * o <= FORGET
        ident, ones, mod, bada, vec = (small[n] for n in ("ident", "ones", "mod", "bada", "vec"))
        cact, a1, a2, wy, wx = (small[n] for n in ("cact", "a1", "a2", "wy", "wx"))
        sinks, sel, bf, eps, ss, rr = (small[n] for n in ("sinks", "sel", "bf", "eps", "ss", "rr"))
        colraw, rowmax, negmax, rowsum = (small[n] for n in ("colraw", "rowmax", "negmax", "rowsum"))
        esink, rinv, sinkcol = (small[n] for n in ("esink", "rinv", "sinkcol"))
        fq_rows = at("fq_rows", FORGET, S, F32R)
        fk_rows = at("fk_rows", FORGET + T, S, F32R)
        cos = at("cos", TAB, S)
        sin = at("sin", TAB + T, S)
        foxmask = at("foxmask", TAB, S)
        swamask = at("swamask", TAB + T, 2 * P)
        ada_acc = at("ada_acc", WORK, 4 * UN)
        ada_acc2 = at("ada_acc2", FORGET, 4 * UN)
        ada_sum = at("ada_sum", WORK + 16 * UN, UN)
        W4 = WORK + 20 * UN
        full = at("full", W4, 4 * S)
        sq = at("sq", W4, 2 * S)
        rs = at("rs", W4 + 2 * T, 2 * S)
        vecrows = at("vecrows", W4, 2 * P)
        rbc = at("rbc", W4 + 3 * T, S)
        diag = at("diag", W4 + 2 * T, S)
        BW = TAB + T + 8 * P
        logits = at("logits", BW, 10 * P)
        pt = at("pt", BW + 40 * P, 10 * P)
        o_rows = at("o_rows", BW + 40 * P, S)
        gst = at("gst", BW + 80 * P, 2 * S)
        q_fox = at("q_fox", BW + 40 * P, S)
        fq_head = at("fq_head", BW + 40 * P + T, S, F32R)
        q_swa = at("q_swa", BW + 80 * P + T, S)
        gates = at("gates", W4, 4 * S)
        fz = at("fz", STORE + 4 * T, 4 * S)

        bank = [ctx.enter_context(nc.psum_tensor(f"bank{b}", [P, S], F32)) for b in range(8)]

        x_fm = nc.dram_tensor("x_fm", [KD, P, S], F32).ap()
        gate_fm = nc.dram_tensor("gate_fm", [2 * KD, P, S], F32).ap()

        raw_landed = [sem(f"raw_landed{s}") for s in range(RING)]
        hi_done, lo_done, unit_done = sem("hi_done"), sem("lo_done"), sem("unit_done")
        ada_mac, ada_summed, ada_cols = sem("ada_mac"), sem("ada_summed"), sem("ada_cols")
        col_copied, mod_ready, scale_ready = sem("col_copied"), sem("mod_ready"), sem("scale_ready")
        const_landed, vec_landed = sem("const_landed"), sem("vec_landed")
        x_landed = [sem(f"x_landed{t}") for t in range(TB)]
        ones_set, vecs_turned, vecs_copied, cact_done = (
            sem("ones_set"), sem("vecs_turned"), sem("vecs_copied"), sem("cact_done"))
        prep = sem("prep")
        x_squared, r_root, r_ready, diag_ready, r_spread, r_copied = (
            sem("x_squared"), sem("r_root"), sem("r_ready"), sem("diag_ready"), sem("r_spread"), sem("r_copied"))
        x_turned, xt_copied, x_spilled, xn_ready = (
            sem("x_turned"), sem("xt_copied"), sem("x_spilled"), sem("xn_ready"))
        h_full, h_hi_done, h_ready = sem("h_full"), sem("h_hi_done"), sem("h_ready")
        act_evicted = sem("act_evicted")
        tab_landed, vec_zeroed, y_rooted, x_rooted = sem("tab_landed"), sem("vec_zeroed"), sem("y_rooted"), sem("x_rooted")
        sink_set, sumsq_zero, a1_step = sem("sink_set"), sem("sumsq_zero"), sem("a1_step")
        f_act, f_dve = sem("f_act"), sem("f_dve")
        y_posts, y_stats, y_chain = sem("y_posts"), sem("y_stats"), sem("y_chain")
        x_posts, x_stats, x_chain = sem("x_posts"), sem("x_stats"), sem("x_chain")
        masks_landed = sem("masks_landed")
        q_copied, fq_done = sem("q_copied"), sem("fq_done")
        s_done, s_stats, negmax_done, p_done, sums_added, rinv_done = (
            sem("s_done"), sem("s_stats"), sem("negmax_done"), sem("p_done"), sem("sums_added"), sem("rinv_done"))
        p_turned, pt_act, pt_dve, pv_done, o_scaled, o_turned, o_hi_done, o_ready = (
            sem("p_turned"), sem("pt_act"), sem("pt_dve"), sem("pv_done"), sem("o_scaled"),
            sem("o_turned"), sem("o_hi_done"), sem("o_ready"))
        gate_spilled, gates_landed = sem("gate_spilled"), sem("gates_landed")
        m_step, m_hi_done, m_ready = sem("m_step"), sem("m_hi_done"), sem("m_ready")
        xr_landed = [sem("xr_landed0"), sem("xr_landed1")]
        x2_done, x2_squared, x2_summed = sem("x2_done"), sem("x2_squared"), sem("x2_summed")
        r2_sum, r2_root, r2_ready, h2_scaled = sem("r2_sum"), sem("r2_root"), sem("r2_ready"), sem("h2_scaled")
        g_act, u_mul, u_hi_done, u_ready = sem("g_act"), sem("u_mul"), sem("u_hi_done"), sem("u_ready")
        acc_done = sem("acc_done")
        o_block_turned, out_copied_a, out_copied_d, out_stored = (
            sem("o_block_turned"), sem("out_copied_a"), sem("out_copied_d"), sem("out_stored"))

        w_in_k = w_in[0].rearrange("(t p) n -> p t n", p=P)
        w_ada_k = w_ada[0].rearrange("(t p) n -> p t n", p=P)
        w_oa_k = w_o_swa[0].rearrange("(t p) n -> p t n", p=P)
        w_of_k = w_o_fox[0].rearrange("(t p) n -> p t n", p=P)
        w_out_k = w_out[0].rearrange("(t p) n -> p t n", p=P)
        w_fi_k = w_ffn_in[0].rearrange("(t p) n -> p t n", p=P)
        w_fo_k = w_ffn_out[0].rearrange("(t p) n -> p t n", p=P)
        x_tb = x[0].rearrange("(t p) n -> t p n", p=P)
        out_tb = out[0].rearrange("(t p) n -> t p n", p=P)

        def tile(t, n, width=S):
            if isinstance(n, int):
                return t[:, n * width:(n + 1) * width]
            return t[:, bass.ds(n * width, width)]

        def col(t, n, k=1):
            return t[:, n:n + k] if isinstance(n, int) else t[:, bass.ds(n, k)]

        def unit(t, u):
            return t[:, (u % RING) * UK * UN:(u % RING + 1) * UK * UN]


        ph_f = dict(r=F_R, n=4, it=1, u=F_U, ada=None)
        ph_y0 = dict(r=Y0_R, n=4, it=1, u=Y0_U, ada=None)
        ph_y1 = dict(r=Y1_R, n=4, it=1, u=Y1_U, ada=None)
        ph_a = dict(r=A_R, n=A_N, it=A_I, u=A_U, ada=ADA_A)
        ph_b = dict(r=B_R, n=B_N, it=B_I, u=B_U, ada=None)
        ph_c = dict(r=C_R, n=C_N, it=C_I, u=C_U, ada=ADA_C)
        ph_d = dict(r=D_R, n=D_N, it=D_I, u=D_U, ada=ADA_D)
        ph_e = dict(r=E_R, n=E_N, it=E_I, u=E_U, ada=None)
        after = {id(a): b for a, b in zip((ph_f, ph_y0, ph_y1, ph_a, ph_b, ph_c, ph_d),
                                          (ph_y0, ph_y1, ph_a, ph_b, ph_c, ph_d, ph_e))}

        def ahead(ph, i, j, last):
            j += LEAD
            if j < ph["n"]:
                return ph, i, j
            if not last:
                return ph, i + 1, j - ph["n"]
            if ph is ph_e:
                return None
            return after[id(ph)], 0, j - ph["n"]

        def numbers(ph, i, j):
            k = 2 if ph["ada"] is not None else 1
            u = ph["u"] + k * j
            return ph["r"] + ph["n"] * i + j, u % RING, u // RING + i * (k * ph["n"] // RING)

        def each(eng, n, body):
            if n > 1:
                with eng.Fori(0, n - 1) as i:
                    body(i, False)
            body(n - 1, True)

        fox_blocks = [list(range(qb + 1)) for qb in range(TB)]
        swa_blocks = [list(range(max(qb - 1, 0), qb + 1)) for qb in range(TB)]

        def starts(blocks):
            n, got = 0, []
            for b in blocks:
                got.append(n)
                n += len(b)
            return got

        fox_at = [(4 + qb, 0) for qb in range(TB)]
        swa_at = [(6, 0), (6, P), (7, 0), (7, 2 * P)]
        fox_pt = [(5, 0), (5, 1), (5, 2), (6, 0), (6, 1), (6, 2), (7, 0), (7, 1), (7, 2), (7, 3)]
        swa_pt = [(6, 0), (6, 1), (6, 2), (7, 0), (7, 1), (7, 2), (7, 3)]

        block = ctx.enter_context(nc.Block())

        @block.sync
        def _(sp):
            sp.dma_start(ident[:], consts[:, 0:P]).then_inc(const_landed, 16)
            sp.wait_ge(vec_zeroed, 1)
            rows = [(c, 0), (norm1_w, KD), (norm2_w, 2 * KD)]
            for v, r0 in rows:
                sp.dma_start(vecrows[r0:r0 + KD, 0:P], v.rearrange("a (r p) -> (a r) p", p=P)).then_inc(vec_landed, 16)
            for n, w in enumerate((swa_q_norm_w, swa_k_norm_w, fox_q_norm_w, fox_k_norm_w)):
                sp.dma_start(vecrows[3 * KD + n:3 * KD + n + 1, 0:P], w).then_inc(vec_landed, 16)
            sp.dma_start(vecrows[0:6 * KD, P:2 * P], b_ada.rearrange("a (r p) -> (a r) p", p=P)).then_inc(vec_landed, 16)
            for tb in range(TB):
                sp.dma_start(x_rows[:, tb * D:(tb + 1) * D], x_tb[tb]).then_inc(x_landed[tb], 16)

            def load(u, src, width=UN):
                dst = unit(w_raw, u).rearrange("p (k n) -> p k n", k=UK)
                sp.dma_start(dst[:, :, 0:width], src).then_inc(raw_landed[u % RING], 32)

            def load_pair(u, kq, col0, col1):
                dst = unit(w_raw, u).rearrange("p (k n) -> p k n", k=UK)
                for t, c0 in enumerate((col0, col1)):
                    sp.dma_start(dst[:, :, t * P:(t + 1) * P],
                                 w_in_k[:, kq * UK:(kq + 1) * UK, bass.ds(c0, P)]).then_inc(raw_landed[u % RING], 16)

            def load_ada(u, kq, c0):
                load(u, w_ada_k[:, kq * UK:(kq + 1) * UK, bass.ds(c0, UN)])

            def split(r):
                sp.wait_ge(lo_done, r + 1)

            def summed(a):
                sp.wait_ge(ada_mac, UK * (a + 1))

            for j in range(STEP):
                load_ada(j, j, D)
            sp.dma_start(cos[:], consts[:, P:P + S]).then_inc(tab_landed, 16)
            sp.dma_start(sin[:], consts[:, P + S:P + 2 * S]).then_inc(tab_landed, 16)
            sp.dma_start(sel[:], consts[:, CONST_W - HQ:CONST_W]).then_inc(tab_landed, 16)
            sp.dma_start(sinks[:], swa_sinks.to_broadcast([P, HQ])).then_inc(tab_landed, 16)
            sp.dma_start(bf[0:HQ, :], b_forget.rearrange("a h -> h a")).then_inc(tab_landed, 16)
            with sp.Fori(0, ADA0_STEPS // 2 - 1) as i:
                for j in range(STEP, 3 * STEP):
                    summed(i * 2 * STEP + j - RING)
                    load_ada(j, j % STEP, i * UN if j < 2 * STEP else (i + 1) * UN + D)
            n0 = 2 * STEP * (ADA0_STEPS // 2 - 1)
            for j in range(STEP, 2 * STEP):
                summed(n0 + j - RING)
                load_ada(j, j % STEP, D - UN)

            for kq in range(4):
                summed(F_U + kq - RING)
                load(F_U + kq, w_in_k[:, kq * UK:(kq + 1) * UK, FL0:FL0 + P], width=P)
            for y in range(KVH):
                for kq in range(4):
                    split(4 * y + kq)
                    load_pair(Y0_U + 4 * y + kq, kq, KA0 + y * P, VA0 + y * P)

            with sp.Fori(0, A_I) as i:
                for j in range(A_N):
                    split(A_R + A_N * i + j - 2)
                    if j < 4:
                        load_pair(A_U + 2 * j, j, (i + QF0 // P) * P, (i + KF0 // P) * P)
                    else:
                        load_pair(A_U + 2 * j, j - 4, QA0 + i * P, VF0 + i * P)
                    summed(STEP * ADA_A + A_N * i + j - 2)
                    load_ada(A_U + 2 * j + 1, j % STEP, (2 * ADA_A + j // STEP * 2) * P + i * 2 * UN)

            summed(STEP * ADA_C - 1)
            split(B_R - 1)
            with sp.Fori(0, B_I) as i:
                for j in range(B_N):
                    split(B_R + B_N * i + j - RING)
                    load(B_U + j, w_in_k[:, (j % 4) * UK:(j % 4 + 1) * UK, bass.ds(G0 + (j // 4) * D + i * UN, UN)])

            split(C_R - 1)
            with sp.Fori(0, C_I) as i:
                for j in range(C_N):
                    split(C_R + C_N * i + j - 2)
                    w = (w_oa_k, w_of_k)[j // 2]
                    load(C_U + 2 * j, w[:, (j % 2) * UK:(j % 2 + 1) * UK, bass.ds(i * UN, UN)])
                    summed(STEP * ADA_C + C_N * i + j - 2)
                    load_ada(C_U + 2 * j + 1, j, 2 * ADA_C * P + i * UN)

            with sp.Fori(0, D_I) as i:
                for j in range(D_N):
                    split(D_R + D_N * i + j - 2)
                    load(D_U + 2 * j, w_out_k[:, (j % 4) * UK:(j % 4 + 1) * UK, bass.ds((j // 4) * UN + i * 2 * UN, UN)])
                    summed(STEP * ADA_D + D_N * i + j - 2)
                    load_ada(D_U + 2 * j + 1, j % STEP, (2 * ADA_D + j // STEP * 2) * P + i * 2 * UN)

            summed(STEP * (ADA_D + 2 * D_I) - 1)
            split(E_R - 1)
            with sp.Fori(0, E_I) as i:
                for j in range(E_N):
                    split(E_R + E_N * i + j - RING)
                    if j < 16:
                        pair, kq = j // 4, j % 4
                        c0 = (pair % 2) * DFF + (pair // 2) * UN
                        load(E_U + j, w_fi_k[:, kq * UK:(kq + 1) * UK, bass.ds(c0 + i * UK * P, UN)])
                    else:
                        load(E_U + j, w_fo_k[:, bass.ds(i * UK, UK), (j - 16) * UN:(j - 15) * UN])

            for m in range(TB * TB):
                tb, n4 = m % TB, m // TB
                sp.wait_ge((out_copied_a, out_copied_d)[m % 2], m // 2 + 1)
                sp.dma_start(out_tb[tb][:, n4 * S:(n4 + 1) * S],
                             out_rows[:, tb * D + n4 * S:tb * D + (n4 + 1) * S]).then_inc(out_stored, 16)
            sp.wait_ge(out_stored, 16 * TB * TB)

        @block.tensor
        def _(pe):
            def gemm(r, slot, hi, lo, k0, banks, first, last, ready=None, reads=None):
                pe.wait_ge(lo_done, r + 1)
                whi, wlo = unit(w_hi, slot), unit(w_lo, slot)
                for k in range(UK):
                    if ready is not None:
                        pe.wait_ge(ready, reads(k0 + k))
                    for t, b in enumerate(banks):
                        cols = slice(k * UN + t * P, k * UN + (t + 1) * P)
                        first_k, last_k = first and k == 0, last and k == UK - 1
                        xh, xl = tile(hi, k0 + k), tile(lo, k0 + k)
                        nc.tensor.matmul(bank[b][:], lhsT=whi[:, cols], rhs=xh, start=first_k, stop=False)
                        nc.tensor.matmul(bank[b][:], lhsT=whi[:, cols], rhs=xl, start=False, stop=False)
                        mm = nc.tensor.matmul(bank[b][:], lhsT=wlo[:, cols], rhs=xh, start=False, stop=last_k)
                mm.then_inc(unit_done, 1)

            def cols_of_step(s):
                pe.wait_ge(ada_summed, s + 3)
                pe.wait_ge(col_copied, s + 1)
                for t in range(2):
                    mm = nc.tensor.matmul(bank[4][:, t:t + 1], lhsT=ada_sum[:, t * P:(t + 1) * P],
                                          rhs=ones[:, 0:1], start=True, stop=True)
                mm.then_inc(ada_cols, 1)

            pe.wait_ge(const_landed, 16)
            pe.wait_ge(ones_set, 1)
            pe.wait_ge(vec_landed, 16 * 8)
            nc.tensor.transpose(bank[5][:, 0:P], vecrows[:, 0:P], ident[:])
            nc.tensor.transpose(bank[5][:, P:2 * P], vecrows[:, P:2 * P], ident[:]).then_inc(vecs_turned, 1)
            for tb in range(TB):
                pe.wait_ge(x_landed[tb], 16)
            for k in range(KD):
                if k >= 4:
                    pe.wait_ge(xt_copied, k - 3)
                for tb in range(TB):
                    mm = nc.tensor.transpose(bank[k % 4][:, tb * P:(tb + 1) * P],
                                             x_rows[:, tb * D + k * P:tb * D + (k + 1) * P], ident[:])
                mm.then_inc(x_turned, 1)
            pe.wait_ge(diag_ready, TB)
            nc.tensor.matmul(bank[6][:], lhsT=ones[:], rhs=diag[:], start=True, stop=True).then_inc(r_spread, 1)
            with pe.Fori(0, ADA0_STEPS // 2) as i:
                cols_of_step(2 * i)
                cols_of_step(2 * i + 1)

            pe.wait_ge(xt_copied, KD)
            for j in range(4):
                gemm(F_R + j, F_R + j, h_hi, h_lo, UK * j, (0,), j == 0, j == 3,
                     h_ready, lambda k: k + 3)

            def y_post(y, evicted):
                pe.wait_ge(act_evicted, evicted)
                pe.wait_ge(y_stats, y + 1)
                nc.tensor.matmul(bank[6][:], lhsT=ones[:], rhs=tile(sq, 0), start=True, stop=True)
                for tb in range(TB):
                    mm = nc.tensor.transpose(bank[7][:, tb * P:(tb + 1) * P],
                                             sq[:, S + tb * P:S + (tb + 1) * P], ident[:])
                mm.then_inc(y_posts, 1)

            for y in range(KVH):
                for j in range(4):
                    if y == 1 and j == 0:
                        pe.wait_ge(act_evicted, 1)
                    gemm(Y0_R + 4 * y + j, Y0_R + 4 * y + j, h_hi, h_lo, UK * j,
                         ((2, 3), (0, 1))[y], j == 0, j == 3)
                    if y == 1 and j == 0:
                        y_post(0, 2)

            with pe.Fori(0, A_I) as i:
                for j in range(A_N):
                    if j == 0:
                        pe.wait_ge(act_evicted, 2 * i + 2)
                    if j == 4:
                        pe.wait_ge(act_evicted, 2 * i + 3)
                    gemm(A_R + A_N * i + j, A_R + j, h_hi, h_lo, UK * (j % 4),
                         ((2, 3), (0, 1))[j // 4], j % 4 == 0, j % 4 == 3)
                    if j == 0:
                        y_post(i + 1, 2 * i + 3)
                    if j == 2:
                        cols_of_step(ADA_A + 2 * i)
                    if j == 4:
                        pe.wait_ge(act_evicted, 2 * i + 4)
                        pe.wait_ge(col_copied, ADA_A + 2 * i + 2)
                        for t in range(2):
                            mm = nc.tensor.matmul(bank[4 + t][:], lhsT=ones[:], rhs=tile(sq, t),
                                                  start=True, stop=True)
                        mm.then_inc(x_posts, 1)
                    if j == 6:
                        pe.wait_ge(x_stats, i + 1)
                        cols_of_step(ADA_A + 2 * i + 1)
            y_post(KVH + HQ - 1, 2 * HQ + 3)

            def probabilities(blocks, where, n):
                pe.wait_ge(p_done, n)
                for b in range(sum(len(x) for x in blocks)):
                    bk, cb = where[b]
                    mm = nc.tensor.transpose(bank[bk][:, cb * P:(cb + 1) * P], logits[:, b * P:(b + 1) * P], ident[:])
                mm.then_inc(p_turned, 1)

            def weighted_values(blocks, v0, n):
                pe.wait_ge(pt_act, n)
                pe.wait_ge(pt_dve, n)
                for qb, b0 in enumerate(starts(blocks)):
                    for m, kb in enumerate(blocks[qb]):
                        v = val[:, bass.ds(v0 + kb * P, P)]
                        mm = nc.tensor.matmul(bank[4][:, qb * P:(qb + 1) * P],
                                              lhsT=pt[:, (b0 + m) * P:(b0 + m + 1) * P], rhs=v,
                                              start=m == 0, stop=m == len(blocks[qb]) - 1)
                mm.then_inc(pv_done, 1)

            def turn_output(n):
                pe.wait_ge(o_scaled, n)
                for qb in range(TB):
                    mm = nc.tensor.transpose(bank[5][:, qb * P:(qb + 1) * P], o_rows[:, qb * P:(qb + 1) * P], ident[:])
                mm.then_inc(o_turned, 1)

            pe.wait_ge(y_stats, KVH + HQ + 1)
            pe.wait_ge(col_copied, ADA_C + 1)
            with pe.Fori(0, B_I) as h:
                for j in range(B_N):
                    if j == 0:
                        pe.wait_ge(act_evicted, 2 * h + 18)
                    if j == 4:
                        pe.wait_ge(act_evicted, 2 * h + 19)
                    gemm(B_R + B_N * h + j, B_R + j, h_hi, h_lo, UK * (j % 4),
                         ((2, 3), (0, 1))[j // 4], j % 4 == 0, j % 4 == 3)
                    if j == 0:
                        pe.wait_ge(q_copied, 2 * h + 1)
                        pe.wait_ge(fq_done, h + 1)
                        pe.wait_ge(o_ready, 2 * h + 2)
                        for qb in range(TB):
                            n = (qb + 1) * P
                            nc.tensor.matmul(bank[4 + qb][:, 0:n], lhsT=q_fox[:, qb * P:(qb + 1) * P],
                                             rhs=kf[:, bass.ds(h * S, n)], start=True, stop=False)
                            mm = nc.tensor.matmul(bank[4 + qb][:, 0:n], lhsT=fq_head[:, qb * P:(qb + 1) * P],
                                                  rhs=fk_rows[:, 0:n], start=False, stop=True)
                        mm.then_inc(s_done, 1)
                    if j == 2:
                        probabilities(fox_blocks, fox_pt, 2 * h + 1)
                    if j == 3:
                        weighted_values(fox_blocks, (h + KVH) * S, 2 * h + 1)
                        pe.wait_ge(q_copied, 2 * h + 2)
                        for qb in range(TB):
                            bk, c0 = swa_at[qb]
                            kb = swa_blocks[qb]
                            mm = nc.tensor.matmul(bank[bk][:, c0:c0 + len(kb) * P],
                                                  lhsT=q_swa[:, qb * P:(qb + 1) * P],
                                                  rhs=rot[:, bass.ds((h // GROUP) * S + kb[0] * P, len(kb) * P)],
                                                  start=True, stop=True)
                        mm.then_inc(s_done, 1)
                    if j == 4:
                        turn_output(2 * h + 1)
                    if j == 5:
                        probabilities(swa_blocks, swa_pt, 2 * h + 2)
                    if j == 6:
                        weighted_values(swa_blocks, (h // GROUP) * S, 2 * h + 2)
                    if j == 7:
                        pe.wait_ge(o_ready, 2 * h + 3)
                        turn_output(2 * h + 2)

            pe.wait_ge(act_evicted, 34)
            with pe.Fori(0, C_I) as i:
                pe.wait_ge(o_ready, 2 * HQ + 2)
                for j in range(C_N):
                    if j == 0:
                        pe.wait_ge(m_step, 6 * i + 2)
                    if j == 2:
                        pe.wait_ge(act_evicted, 35)
                        pe.wait_ge(m_step, 6 * i + 4)
                    hi, lo = ((oa_hi, oa_lo), (of_hi, of_lo))[j // 2]
                    gemm(C_R + C_N * i + j, C_R + j, hi, lo, UK * (j % 2),
                         ((2, 3), (0, 1))[j // 2], j % 2 == 0, j % 2 == 1)
                    if j == 1:
                        cols_of_step(ADA_C + i)

            with pe.Fori(0, D_I) as i:
                for j in range(D_N):
                    if j % 4 == 0:
                        pe.wait_ge(m_step, 6 * C_I + 2 + j // 2)
                        pe.wait_ge(x2_done, 4 * i + j // 2 + 2)
                    gemm(D_R + D_N * i + j, D_R + j, h_hi, h_lo, UK * (j % 4),
                         ((2, 3), (0, 1))[j // 4], j % 4 == 0, j % 4 == 3,
                         m_ready if j < 4 else None, lambda k: k + 3)
                    if j in (2, 6):
                        cols_of_step(ADA_D + 2 * i + j // 4)
            pe.wait_ge(x2_summed, KD + 2)
            pe.wait_ge(col_copied, ADA_D + 2 * D_I + 1)
            nc.tensor.matmul(bank[4][:], lhsT=ones[:], rhs=sumsq[:], start=True, stop=True).then_inc(r2_sum, 1)

            with pe.Fori(0, E_I) as i:
                waits = [(acc_done, 7, 8), (acc_done, 8, 8), (act_evicted, 36, 2), (u_mul, 2, 4),
                         (act_evicted, 37, 2), (u_mul, 4, 4)] + [(acc_done, 9 + n, 8) for n in range(6)]
                for q in range(12):
                    s0, n0, step0 = waits[q]
                    pe.wait_ge(s0, i * step0 + n0)
                    banks = ((2, 3), (0, 1))[q % 2]
                    if q < 4:
                        for j in range(4 * q, 4 * q + 4):
                            gemm(E_R + E_N * i + j, E_R + j, h_hi, h_lo, UK * (j % 4), banks, j % 4 == 0,
                                 j % 4 == 3, h_ready if q == 0 else None, lambda k: KD + k + 3)
                    else:
                        j = 12 + q
                        gemm(E_R + E_N * i + j, E_R + j, u_hi, u_lo, 0, banks, True, True,
                             u_ready if q == 4 else None, lambda k: i * UK + k + 1)

            for m in range(TB * TB):
                n4, tb = m // TB, m % TB
                if tb == 0:
                    pe.wait_ge(acc_done, 8 * E_I + (2 * n4 + 2 if n4 == 0 else 8))
                if m >= 8:
                    pe.wait_ge((out_copied_a, out_copied_d)[m % 2], (m - 8) // 2 + 1)
                for q in range(TB):
                    f0 = (n4 * TB + q) * S + tb * P
                    mm = nc.tensor.transpose(bank[(m + 4) % 8][:, q * P:(q + 1) * P], x2[:, f0:f0 + P], ident[:])
                mm.then_inc(o_block_turned, 1)

        @block.scalar
        def _(act):
            def split(ph, i, j, last):
                at_ = ahead(ph, i, j, last)
                if at_ is None:
                    return
                r, slot, use = numbers(*at_)
                act.wait_ge(raw_landed[slot], use * 32 + 32)
                if not isinstance(r, int) or r >= RING:
                    act.wait_ge(unit_done, r - RING + 1)
                ws = numbers(at_[0], 0, at_[2])[0] % RING
                n = P if at_[0] is ph_f else UN
                view = [unit(t, s).rearrange("p (k n) -> p k n", k=UK)[:, :, 0:n]
                        for t, s in ((w_raw, slot), (w_hi, ws))]
                nc.scalar.activation(view[1], view[0], ACT.Copy).then_inc(hi_done, 1)

            def copy_cols(s):
                act.wait_ge(ada_cols, s + 2)
                act.wait_ge(mod_ready, s + 1)
                nc.scalar.activation(colraw[:], bank[4][:, 0:2], ACT.Copy).then_inc(col_copied, 1)

            act.wait_ge(vecs_copied, 1)
            nc.scalar.activation(cact[:], vec[:, 0:KD], ACT.Silu).then_inc(cact_done, 1)
            for tb in range(TB):
                act.wait_ge(x_landed[tb], 16)
                if tb:
                    act.wait_ge(x_squared, tb)
                nc.scalar.activation(junk[:], x_rows[:, tb * D:(tb + 1) * D], ACT.Square,
                                     accum_out=ss[:, tb:tb + 1]).then_inc(x_squared, 1)
            act.wait_ge(x_squared, TB)
            nc.scalar.activation(rr[:], ss[:], ACT.Sqrt, bias=eps[:], scale=1.0 / D).then_inc(r_root, 1)
            for k in range(KD):
                act.wait_ge(x_turned, k + 1)
                nc.scalar.activation(tile(xn, k), bank[k % 4][:], ACT.Copy).then_inc(xt_copied, 1)
                if k % 4 == 3:
                    act.wait_ge(xt_copied, k + 1)
                    act.dma_start(x_fm[k - 3:k + 1].rearrange("k p s -> p k s"),
                                  xn[:, (k - 3) * S:(k + 1) * S].rearrange("p (k s) -> p k s", k=4)
                                  ).then_inc(x_spilled, 16)
            act.wait_ge(r_spread, 1)
            nc.scalar.activation(rbc[:], bank[6][:], ACT.Copy).then_inc(r_copied, 1)

            def h_tile(n, k, t, src, a, b, whole):
                act.wait_ge(h_ready, n + 1)
                nc.scalar.activation(tile(whole, t), src, ACT.Identity, scale=a, bias=b).then_inc(h_full, 1)
                act.wait_ge(h_full, n + 1)
                nc.scalar.activation(tile(h_hi, k), tile(whole, t), ACT.Copy).then_inc(h_hi_done, 1)

            with act.Fori(0, ADA0_STEPS // 2) as i:
                copy_cols(2 * i)
                copy_cols(2 * i + 1)
                act.wait_ge(xn_ready, 2 * i + 2)
                act.wait_ge(mod_ready, 2 * i + 3)
                act.wait_ge(scale_ready, i + 1)
                for t in range(2):
                    h_tile(2 * i + t, 2 * i + t, t, tile(xn, 2 * i + t), col(a1, 2 * i + t), col(mod, 2 * i + t), full)

            for j in range(LEAD):
                split(ph_f, 0, j - LEAD, False)
            for j in range(4):
                split(ph_f, 0, j, True)
            act.wait_ge(unit_done, F_R + 4)
            act.wait_ge(tab_landed, 16 * 5)
            nc.scalar.activation(fz[0:HQ, 0:S], bank[0][0:HQ, :], ACT.Identity, bias=bf[0:HQ, :]).then_inc(act_evicted, 1)
            act.wait_ge(f_dve, 1)
            nc.scalar.activation(fz[0:HQ, 2 * S:3 * S], fz[0:HQ, S:2 * S], ACT.Exp).then_inc(f_act, 1)
            act.wait_ge(f_act, 1)
            nc.scalar.activation(fz[0:HQ, 3 * S:4 * S], fz[0:HQ, 2 * S:3 * S], ACT.Ln, bias=ones[0:HQ, 0:1]).then_inc(f_act, 1)

            def y_evict(y, b):
                nc.scalar.activation(tile(sq, 0), bank[b][:], ACT.Square)
                nc.scalar.activation(tile(rot, y), bank[b][:], ACT.Copy)
                nc.scalar.activation(tile(sq, 1), bank[b + 1][:], ACT.Copy).then_inc(act_evicted, 1)

            def y_roots(y):
                act.wait_ge(y_posts, y + 1)
                nc.scalar.activation(tile(rs, 0), bank[6][:], ACT.Sqrt, bias=eps[:], scale=1.0 / DH).then_inc(y_rooted, 1)
                nc.scalar.activation(tile(val, y), bank[7][:], ACT.Copy).then_inc(y_stats, 1)

            for j in range(4):
                split(ph_y0, 0, j, True)
            act.wait_ge(unit_done, Y0_R + 4)
            y_evict(0, 2)
            for j in range(4):
                split(ph_y1, 0, j, True)
                if j == 1:
                    y_roots(0)
            act.wait_ge(unit_done, Y1_R + 4)
            y_evict(1, 0)

            def heads(i, last):
                for j in range(A_N):
                    split(ph_a, i, j, last)
                    if j == 1:
                        act.wait_ge(x_chain, 4 * i + 4)
                        act.wait_ge(y_chain, 6 * i + 6)
                        y_roots(i + 1)
                    if j == 3:
                        copy_cols(ADA_A + 2 * i)
                    if j == 4:
                        act.wait_ge(unit_done, A_R + A_N * i + 4)
                        nc.scalar.activation(tile(sq, 0), bank[2][:], ACT.Square)
                        nc.scalar.activation(tile(sq, 1), bank[3][:], ACT.Square)
                        nc.scalar.activation(tile(qf, i), bank[2][:], ACT.Copy)
                        nc.scalar.activation(tile(kf, i), bank[3][:], ACT.Copy).then_inc(act_evicted, 1)
                    if j == 5:
                        act.wait_ge(x_posts, i + 1)
                        act.wait_ge(y_chain, 6 * i + 12)
                        for t in range(2):
                            nc.scalar.activation(tile(rs, t), bank[4 + t][:], ACT.Sqrt, bias=eps[:],
                                                 scale=1.0 / DH).then_inc(x_stats if t else x_rooted, 1)
                    if j == 7:
                        copy_cols(ADA_A + 2 * i + 1)
                act.wait_ge(unit_done, A_R + A_N * i + 8)
                y_evict(i + KVH, 0)
            each(act, A_I, heads)
            act.wait_ge(x_chain, 4 * A_I + 4)
            act.wait_ge(y_chain, 6 * (KVH + HQ - 1))
            y_roots(KVH + HQ - 1)

            def exponentials(blocks, n, h=None):
                act.wait_ge(negmax_done, n)
                for qb, b0 in enumerate(starts(blocks)):
                    w = slice(b0 * P, (b0 + len(blocks[qb])) * P)
                    ex = nc.scalar.activation(logits[:, w], logits[:, w], ACT.Exp, bias=negmax[:, qb:qb + 1],
                                              accum_out=rowsum[:, qb:qb + 1])
                if h is not None:
                    ex = nc.scalar.activation(esink[:], negmax[:], ACT.Exp, bias=sinkcol[:])
                ex.then_inc(p_done, 1)

            def gate(b, n):
                for t in range(2):
                    g = nc.scalar.activation(tile(gst, t), bank[b + t][:], ACT.Sigmoid)
                g.then_inc(act_evicted, 1)

            def head_pair(h, last):
                for j in range(B_N):
                    split(ph_b, h, j, last)
                    if j == 1:
                        exponentials(fox_blocks, 2 * h + 1)
                    if j == 3:
                        act.wait_ge(p_turned, 2 * h + 1)
                        nc.scalar.activation(pt[:, 0:3 * P], bank[5][:, 0:3 * P], ACT.Copy)
                        nc.scalar.activation(pt[:, 3 * P:6 * P], bank[6][:, 0:3 * P], ACT.Copy).then_inc(pt_act, 1)
                    if j == 4:
                        exponentials(swa_blocks, 2 * h + 2, h)
                        act.wait_ge(unit_done, B_R + B_N * h + 4)
                        gate(2, 0)
                    if j == 5:
                        act.wait_ge(o_turned, 2 * h + 3)
                        nc.scalar.activation(tile(of_hi, h), bank[5][:], ACT.Copy).then_inc(o_hi_done, 1)
                    if j == 6:
                        act.wait_ge(p_turned, 2 * h + 2)
                        nc.scalar.activation(pt[:, 0:3 * P], bank[6][:, 0:3 * P], ACT.Copy).then_inc(pt_act, 1)
                act.wait_ge(o_turned, 2 * h + 4)
                nc.scalar.activation(tile(oa_hi, h), bank[5][:], ACT.Copy).then_inc(o_hi_done, 1)
                act.wait_ge(unit_done, B_R + B_N * h + 8)
                act.wait_ge(gate_spilled, 32 * h + 16)
                gate(0, 1)
            each(act, B_I, head_pair)

            def merge(i, last):
                for j in range(C_N):
                    split(ph_c, i, j, last)
                    if j == 2:
                        copy_cols(ADA_C + i)
                act.wait_ge(m_step, 6 * i + 12)
                for t in range(2):
                    nc.scalar.activation(tile(h_hi, 2 * i + t), tile(gates, t), ACT.Copy).then_inc(m_hi_done, 1)
            each(act, C_I, merge)

            def project(i, last):
                for j in range(D_N):
                    split(ph_d, i, j, last)
                    if j in (3, 7):
                        copy_cols(ADA_D + 2 * i + j // 4)
                    if j == 4:
                        squares(2 * i)
                squares(2 * i + 1)

            def squares(d):
                act.wait_ge(x2_done, 2 * d + 6)
                act.wait_ge(x2_summed, 2 * d + 2)
                for t in range(2):
                    nc.scalar.activation(tile(sq2, t), tile(x2, 2 * d + t), ACT.Square).then_inc(x2_squared, 1)
            each(act, D_I, project)
            act.wait_ge(r2_sum, 1)
            nc.scalar.activation(r2[:], bank[4][:], ACT.Sqrt, bias=eps[:], scale=1.0 / D).then_inc(r2_root, 1)
            act.wait_ge(mod_ready, 6 * KD // 2 + 1)
            for k in range(KD):
                act.wait_ge(h2_scaled, k + 1)
                h_tile(KD + k, k, k % 2, tile(h2_t, k % 2), a2[:, k:k + 1],
                       mod[:, 3 * KD + k:3 * KD + k + 1], h2_full)

            def ffn(i, last):
                for j in range(E_N):
                    split(ph_e, i, j, last)
                    if j in (4, 12):
                        act.wait_ge(unit_done, E_R + E_N * i + j)
                        if j == 12:
                            act.wait_ge(u_mul, 4 * i + 2)
                        for t in range(2):
                            g = nc.scalar.activation(tile(sg, t), bank[2 + t][:], ACT.Silu)
                        g.then_inc(act_evicted, 1)
                    if j in (8, 16):
                        for t in range(2):
                            n = (j - 8) // 4 + t
                            act.wait_ge(u_mul, 4 * i + n + 1)
                            nc.scalar.activation(tile(u_hi, n), tile(u_full, t), ACT.Copy).then_inc(u_hi_done, 1)
            each(act, E_I, ffn)

            for m in range(TB * TB):
                if m % 2 == 0:
                    act.wait_ge(o_block_turned, m + 1)
                    tb, n4 = m % TB, m // TB
                    nc.scalar.activation(out_rows[:, tb * D + n4 * S:tb * D + (n4 + 1) * S], bank[(m + 4) % 8][:],
                                         ACT.Copy).then_inc(out_copied_a, 1)

        @block.vector
        def _(dve):
            v = nc.vector

            def split(ph, i, j, last):
                at_ = ahead(ph, i, j, last)
                if at_ is None:
                    return
                r, slot, use = numbers(*at_)
                dve.wait_ge(hi_done, r + 1)
                ws = numbers(at_[0], 0, at_[2])[0] % RING
                n = P if at_[0] is ph_f else UN
                raw, hi, lo = [unit(t, s).rearrange("p (k n) -> p k n", k=UK)[:, :, 0:n]
                               for t, s in ((w_raw, slot), (w_hi, ws), (w_lo, ws))]
                v.tensor_tensor(lo, raw, hi.bitcast(F32), ALU.subtract).then_inc(lo_done, 1)
                p, ii, jj = at_
                if p["ada"] is not None:
                    acc = ada_acc if p is ph_a else ada_acc2
                    mac(p["ada"] + p["n"] // STEP * ii + jj // STEP, jj % STEP, p["u"] + 2 * jj + 1,
                        ii * (2 * p["n"] // RING), acc, jj // STEP % 2, p is not ph_a)

            def mac(s, kq, u, uses, accs, s_set, strict):
                dve.wait_ge(raw_landed[u % RING], (u // RING + uses) * 32 + 32)
                w = unit(w_raw, u)
                for k in range(UK):
                    acc = accs[:, (2 * s_set + k % 2) * UN:(2 * s_set + k % 2 + 1) * UN]
                    wk, ck = w[:, k * UN:(k + 1) * UN], cact[:, kq * UK + k:kq * UK + k + 1]
                    if kq == 0 and k < 2:
                        if k == 0:
                            dve.wait_ge(ada_summed, s + (2 if strict else 1))
                        v.tensor_scalar(acc, wk, ck, None, ALU.mult).then_inc(ada_mac, 1)
                    else:
                        dve.wait_ge(ada_mac, s * STEP * UK + kq * UK + k - 1)
                        v.scalar_tensor_tensor(out=acc, in0=wk, scalar=ck, in1=acc, op0=ALU.mult,
                                               op1=ALU.add).then_inc(ada_mac, 1)

            v.memset(vecrows[:], 0.0).then_inc(vec_zeroed, 1)
            v.memset(eps[:], EPS)
            v.memset(ones[:], 1.0).then_inc(ones_set, 1)
            dve.wait_ge(vecs_turned, 1)
            v.tensor_copy(vec[:], bank[5][:, 0:64]).then_inc(vecs_copied, 1)
            v.tensor_copy(bada[:], bank[5][:, P:P + 6 * KD]).then_inc(vecs_copied, 1)
            dve.wait_ge(vecs_copied, 2)
            n0 = 3 * KD
            v.tensor_scalar(wy[:, 0:KVH], ones[:, 0:KVH], vec[:, n0 + 1:n0 + 2], None, ALU.mult)
            v.tensor_scalar(wy[:, KVH:KVH + HQ], ones[:, 0:HQ], vec[:, n0:n0 + 1], SCALE, ALU.mult, ALU.mult)
            v.tensor_scalar(wx[:, 0:1], ones[:, 0:1], vec[:, n0 + 2:n0 + 3], SCALE, ALU.mult, ALU.mult)
            v.tensor_copy(wx[:, 1:2], vec[:, n0 + 3:n0 + 4]).then_inc(prep, 1)
            dve.wait_ge(r_root, 1)
            v.reciprocal(rr[:], rr[:]).then_inc(r_ready, 1)
            dve.wait_ge(r_ready, 1)
            for tb in range(TB):
                v.tensor_scalar(diag[:, tb * P:(tb + 1) * P], ident[:], rr[:, tb:tb + 1], None,
                                ALU.mult).then_inc(diag_ready, 1)
            dve.wait_ge(cact_done, 1)
            with dve.Fori(0, ADA0_STEPS // 2) as i:
                for j in range(2 * STEP):
                    mac(2 * i + j // STEP, j % STEP, j, i * (2 * STEP // RING), ada_acc, j // STEP, False)

            for j in range(LEAD):
                split(ph_f, 0, j - LEAD, False)
            for j in range(4):
                split(ph_f, 0, j, True)
            f = [fz[0:HQ, n * S:(n + 1) * S] for n in range(4)]
            dve.wait_ge(act_evicted, 1)
            v.scalar_tensor_tensor(out=f[1], in0=f[0], scalar=-1.0, in1=f[0], op0=ALU.mult,
                                   op1=ALU.min).then_inc(f_dve, 1)
            dve.wait_ge(f_act, 2)
            v.scalar_tensor_tensor(out=f[2], in0=f[0], scalar=0.0, in1=f[3], op0=ALU.min,
                                   op1=ALU.subtract).then_inc(f_dve, 1)
            dve.wait_ge(f_dve, 2)
            v.memset(f[0], 1.0).then_inc(f_dve, 1)
            dve.wait_ge(f_dve, 3)
            v.tensor_tensor_scan(f[1], f[0], f[2], 0.0, ALU.mult, ALU.add).then_inc(f_dve, 1)
            v.memset(fq_rows[:].bitcast(F32), 0.0)
            v.memset(fk_rows[:].bitcast(F32), 0.0).then_inc(f_dve, 1)
            dve.wait_ge(f_dve, 5)
            for r0 in (64, 96):
                v.memset(fq_rows[r0:r0 + HQ, :].bitcast(F32), 1.0)
            for r0 in (0, 32):
                v.memset(fk_rows[r0:r0 + HQ, :].bitcast(F32), 1.0)
            v.tensor_copy(fq_rows[0:HQ, :], f[1]).then_inc(f_dve, 1)
            dve.wait_ge(f_dve, 6)
            v.tensor_tensor(f[2], f[1], fq_rows[0:HQ, :].bitcast(F32), ALU.subtract).then_inc(f_dve, 1)
            dve.wait_ge(f_dve, 7)
            v.tensor_copy(fq_rows[32:32 + HQ, :], f[2])
            v.tensor_scalar(fk_rows[64:64 + HQ, :], fq_rows[0:HQ, :].bitcast(F32), -1.0, None, ALU.mult)
            v.tensor_scalar(fk_rows[96:96 + HQ, :], f[2], -1.0, None, ALU.mult).then_inc(f_dve, 1)

            def y_norm(y):
                hd, r0, tmp = tile(rot, y), tile(rs, 0), tile(rs, 1)
                n = 6 * y
                half = DH // 2
                dve.wait_ge(y_rooted, y + 1)
                v.reciprocal(r0, r0).then_inc(y_chain, 1)
                dve.wait_ge(y_chain, n + 1)
                v.scalar_tensor_tensor(out=hd, in0=hd, scalar=col(wy, y), in1=r0, op0=ALU.mult,
                                       op1=ALU.mult).then_inc(y_chain, 1)
                dve.wait_ge(y_chain, n + 2)
                v.tensor_tensor(tmp[0:half], hd[half:DH], sin[half:DH, :], ALU.mult).then_inc(y_chain, 1)
                v.tensor_tensor(tmp[half:DH], hd[0:half], sin[0:half, :], ALU.mult).then_inc(y_chain, 1)
                dve.wait_ge(y_chain, n + 4)
                v.tensor_tensor(hd, hd, cos[:], ALU.mult).then_inc(y_chain, 1)
                dve.wait_ge(y_chain, n + 5)
                v.tensor_tensor(hd, hd, tmp, ALU.add).then_inc(y_chain, 1)

            for j in range(4):
                split(ph_y0, 0, j, True)
            for j in range(4):
                split(ph_y1, 0, j, True)
                if j == 1:
                    dve.wait_ge(tab_landed, 16 * 5)
                    y_norm(0)

            def heads(i, last):
                for j in range(A_N):
                    split(ph_a, i, j, last)
                    if j == 1:
                        y_norm(i + 1)
                    if j == 5:
                        for t, hd in enumerate((qf, kf)):
                            dve.wait_ge((x_rooted, x_stats)[t], i + 1)
                            v.reciprocal(tile(rs, t), tile(rs, t)).then_inc(x_chain, 1)
                        for t, hd in enumerate((qf, kf)):
                            dve.wait_ge(x_chain, 4 * i + 4 + t + 1)
                            v.scalar_tensor_tensor(out=tile(hd, i), in0=tile(hd, i), scalar=wx[:, t:t + 1],
                                                   in1=tile(rs, t), op0=ALU.mult, op1=ALU.mult).then_inc(x_chain, 1)
            each(dve, A_I, heads)
            y_norm(KVH + HQ - 1)

            def masked(blocks, where, mask, n, stats, h=None):
                if h is not None:
                    dve.wait_ge(sink_set, h + 1)
                dve.wait_ge(s_done, n)
                v.memset(negmax[:], 0.0)
                for qb, b0 in enumerate(starts(blocks)):
                    bk, c0 = where[qb]
                    w = len(blocks[qb]) * P
                    wide = mask.shape[1]
                    v.tensor_tensor_reduce(out=logits[:, b0 * P:b0 * P + w], in0=bank[bk][:, c0:c0 + w],
                                           in1=mask[:, wide - w:wide], scale=1.0, scalar=-3.0e38, op0=ALU.add,
                                           op1=ALU.max, accum_out=rowmax[:, qb:qb + 1]).then_inc(s_stats, 1)
                dve.wait_ge(s_stats, stats)
                if h is None:
                    v.tensor_scalar(negmax[:], rowmax[:], -1.0, None, ALU.mult).then_inc(negmax_done, 1)
                else:
                    v.tensor_scalar(negmax[:], rowmax[:], sinkcol[:], -1.0, ALU.max, ALU.mult).then_inc(negmax_done, 1)

            def scale_output(n):
                dve.wait_ge(pv_done, n)
                dve.wait_ge(rinv_done, n)
                v.tensor_tensor(o_rows[:].rearrange("p (q d) -> p q d", q=TB),
                                bank[4][:].rearrange("p (q d) -> p q d", q=TB),
                                rinv[:].rearrange("p (q a) -> p q a", a=1).to_broadcast([P, TB, P]),
                                ALU.mult).then_inc(o_scaled, 1)

            def low_output(dst, hi, n):
                dve.wait_ge(o_hi_done, n)
                v.tensor_tensor(dst, bank[5][:], hi.bitcast(F32), ALU.subtract).then_inc(o_ready, 1)

            dve.wait_ge(masks_landed, 32)
            dve.wait_ge(f_dve, 8)

            def head_pair(h, last):
                v.tensor_copy(sinkcol[:], col(sinks, h)).then_inc(sink_set, 1)
                dve.wait_ge(o_turned, 2 * h + 2)
                v.tensor_scalar(fq_head[:], fq_rows[:].bitcast(F32), col(sel, h), None, ALU.mult).then_inc(fq_done, 1)
                for j in range(B_N):
                    split(ph_b, h, j, last)
                    if j == 1:
                        masked(fox_blocks, fox_at, foxmask, 2 * h + 1, 8 * h + 4)
                    if j == 3:
                        dve.wait_ge(p_done, 2 * h + 1)
                        v.reciprocal(rinv[:], rowsum[:]).then_inc(rinv_done, 1)
                        dve.wait_ge(p_turned, 2 * h + 1)
                        v.tensor_copy(pt[:, 6 * P:10 * P], bank[7][:]).then_inc(pt_dve, 1)
                    if j == 4:
                        scale_output(2 * h + 1)
                        masked(swa_blocks, swa_at, swamask, 2 * h + 2, 8 * h + 8, h)
                    if j == 5:
                        low_output(tile(of_lo, h), tile(of_hi, h), 2 * h + 1)
                        dve.wait_ge(p_done, 2 * h + 2)
                        v.tensor_tensor(rowsum[:], rowsum[:], esink[:], ALU.add).then_inc(sums_added, 1)
                        dve.wait_ge(sums_added, h + 1)
                        v.reciprocal(rinv[:], rowsum[:]).then_inc(rinv_done, 1)
                    if j == 6:
                        dve.wait_ge(p_turned, 2 * h + 2)
                        v.tensor_copy(pt[:, 3 * P:7 * P], bank[7][:]).then_inc(pt_dve, 1)
                    if j == 7:
                        scale_output(2 * h + 2)
                low_output(tile(oa_lo, h), tile(oa_hi, h), 2 * h + 2)
            each(dve, B_I, head_pair)

            def merge(i, last):
                def gated(t4, b):
                    v.tensor_tensor(tile(gates, t4), bank[b][:], tile(gates, t4), ALU.mult).then_inc(m_step, 1)

                for j in range(C_N):
                    split(ph_c, i, j, last)
                    if j == 2:
                        dve.wait_ge(unit_done, C_R + C_N * i + 2)
                        dve.wait_ge(gates_landed, 32 * i + 32)
                        gated(0, 2)
                        gated(1, 3)
                dve.wait_ge(unit_done, C_R + C_N * i + 4)
                gated(2, 0)
                gated(3, 1)
                dve.wait_ge(m_step, 6 * i + 10)
                for t in range(2):
                    v.tensor_tensor(tile(gates, t), tile(gates, t), tile(gates, 2 + t), ALU.add).then_inc(m_step, 1)
                for t in range(2):
                    dve.wait_ge(m_hi_done, 2 * i + t + 1)
                    v.tensor_tensor(tile(h_lo, 2 * i + t), tile(gates, t), tile(h_hi, 2 * i + t).bitcast(F32),
                                    ALU.subtract).then_inc(m_ready, 1)
            each(dve, C_I, merge)

            def residual(i, q):
                d = 2 * i + q
                dve.wait_ge(unit_done, D_R + D_N * i + 4 * q + 4)
                dve.wait_ge(xr_landed[q], 16 * i + 16)
                for t in range(2):
                    v.scalar_tensor_tensor(out=tile(x2, 2 * d + t), in0=bank[(2, 0)[q] + t][:],
                                           scalar=col(mod, 2 * KD + 2 * d + t), in1=tile(xr, 2 * q + t),
                                           op0=ALU.mult, op1=ALU.add).then_inc(x2_done, 1)

            def project(i, last):
                for j in range(D_N):
                    split(ph_d, i, j, last)
                    if j == 4:
                        residual(i, 0)
                residual(i, 1)
            dve.wait_ge(mod_ready, ADA_C + 1)
            each(dve, D_I, project)
            dve.wait_ge(mod_ready, 3 * KD + 1)
            v.scalar_tensor_tensor(out=a2[:], in0=mod[:, 4 * KD:5 * KD], scalar=1.0, in1=vec[:, 2 * KD:3 * KD],
                                   op0=ALU.add, op1=ALU.mult)
            dve.wait_ge(r2_root, 1)
            v.reciprocal(r2[:], r2[:]).then_inc(r2_ready, 1)
            dve.wait_ge(r2_ready, 1)
            for k in range(KD):
                if k >= 2:
                    dve.wait_ge(h_full, KD + k - 1)
                v.tensor_tensor(tile(h2_t, k % 2), tile(x2, k), r2[:], ALU.mult).then_inc(h2_scaled, 1)

            def ffn(i, last):
                for j in range(E_N):
                    split(ph_e, i, j, last)
                    if j in (8, 16):
                        dve.wait_ge(unit_done, E_R + E_N * i + j)
                        dve.wait_ge(act_evicted, 2 * i + 36 + (j - 8) // 8)
                        for t in range(2):
                            v.tensor_tensor(tile(u_full, t), bank[t][:], tile(sg, t), ALU.mult).then_inc(u_mul, 1)
                        for t in range(2):
                            n = (j - 8) // 4 + t
                            dve.wait_ge(u_hi_done, 4 * i + n + 1)
                            v.tensor_tensor(tile(u_lo, n), tile(u_full, t), tile(u_hi, n).bitcast(F32),
                                            ALU.subtract).then_inc(u_ready, 1)
                    if j > 16:
                        accumulate(i, j - 17)
                accumulate(i, 7)

            def accumulate(i, q):
                dve.wait_ge(unit_done, E_R + E_N * i + 17 + q)
                for t in range(2):
                    n = 2 * q + t
                    ins = v.scalar_tensor_tensor(out=tile(x2, n), in0=bank[(2, 0)[q % 2] + t][:],
                                                 scalar=mod[:, 5 * KD + n:5 * KD + n + 1], in1=tile(x2, n),
                                                 op0=ALU.mult, op1=ALU.add)
                ins.then_inc(acc_done, 1)
            each(dve, E_I, ffn)

            for m in range(TB * TB):
                if m % 2 == 1:
                    dve.wait_ge(o_block_turned, m + 1)
                    tb, n4 = m % TB, m // TB
                    v.tensor_copy(out_rows[:, tb * D + n4 * S:tb * D + (n4 + 1) * S],
                                  bank[(m + 4) % 8][:]).then_inc(out_copied_d, 1)

        @block.gpsimd
        def _(pool):
            g = nc.gpsimd
            pool.sem_inc(ada_summed, 2)
            for s in (ada_cols, col_copied, mod_ready, y_stats):
                pool.sem_inc(s, 1)
            for s in (h_ready, o_turned, o_ready, m_ready, x2_summed):
                pool.sem_inc(s, 2)
            pool.sem_inc(x_chain, 4)
            pool.sem_inc(x2_done, 4)
            pool.sem_inc(m_step, 6)
            pool.sem_inc(acc_done, 8)

            def step(s, accs, s_set, ct):
                pool.wait_ge(ada_mac, s * (STEP * UK) + STEP * UK)
                pool.wait_ge(ada_cols, s + 1)
                even, odd = (accs[:, (2 * s_set + n) * UN:(2 * s_set + n + 1) * UN] for n in range(2))
                g.tensor_tensor(ada_sum[:], even, odd, ALU.add).then_inc(ada_summed, 1)
                pool.wait_ge(col_copied, s + 2)
                g.tensor_tensor(col(mod, ct, 2), colraw[:], col(bada, ct, 2), ALU.add).then_inc(mod_ready, 1)

            pool.wait_ge(x_spilled, 16 * 4)
            pool.wait_ge(r_copied, 1)

            def low(k, t, kk, fl):
                pool.wait_ge(h_hi_done, k + 1)
                g.tensor_tensor(tile(h_lo, kk), tile(fl, t), tile(h_hi, kk).bitcast(F32),
                                ALU.subtract).then_inc(h_ready, 1)

            with pool.Fori(0, ADA0_STEPS // 2) as i:
                for t in range(2):
                    g.tensor_tensor(tile(xn, 2 * i + t), tile(xn, 2 * i + t), rbc[:], ALU.mult).then_inc(xn_ready, 1)
                step(2 * i, ada_acc, 0, 2 * i + KD)
                pool.wait_ge(mod_ready, 2 * i + 2)
                g.tensor_tensor(col(a1, 2 * i, 2), col(mod, 2 * i + KD, 2), ones[:, 0:2], ALU.add).then_inc(a1_step, 1)
                pool.wait_ge(a1_step, i + 1)
                g.tensor_tensor(col(a1, 2 * i, 2), col(a1, 2 * i, 2), col(vec, 2 * i + KD, 2),
                                ALU.mult).then_inc(scale_ready, 1)
                step(2 * i + 1, ada_acc, 1, 2 * i)
                for t in range(2):
                    low(2 * i + t, t, 2 * i + t, full)

            with pool.Fori(0, A_I) as i:
                for q in range(2):
                    step(ADA_A + 2 * i + q, ada_acc, q, 2 * ADA_A + 4 * i + 2 * q)

            pool.wait_ge(y_chain, 6 * (KVH + HQ))
            pool.wait_ge(x_chain, 4 * HQ + 4)
            c0 = P + 2 * S
            pool.dma_start(foxmask[:], consts[:, c0:c0 + S]).then_inc(masks_landed, 16)
            pool.dma_start(swamask[:], consts[:, c0 + S:c0 + S + 2 * P]).then_inc(masks_landed, 16)
            g.tensor_copy(q_fox[:], tile(qf, 0)).then_inc(q_copied, 1)
            g.tensor_copy(q_swa[:], tile(rot, KVH)).then_inc(q_copied, 1)

            def spills(h, last):
                for q in range(2):
                    pool.wait_ge(act_evicted, 2 * h + 20 + q)
                    pool.dma_start(gate_fm[bass.ds(2 * h + q * KD, 2)].rearrange("k p s -> p k s"),
                                   gst[:].rearrange("p (k s) -> p k s", k=2)).then_inc(gate_spilled, 16)
                if not last:
                    pool.wait_ge(o_turned, 2 * h + 4)
                    g.tensor_copy(q_fox[:], tile(qf, h + 1)).then_inc(q_copied, 1)
                    pool.wait_ge(gate_spilled, 32 * h + 32)
                    g.tensor_copy(q_swa[:], tile(rot, h + 1 + KVH)).then_inc(q_copied, 1)
            each(pool, B_I, spills)

            pool.wait_ge(gate_spilled, 32 * B_I)
            with pool.Fori(0, C_I) as i:
                step(ADA_C + i, ada_acc2, 0, 2 * ADA_C + 2 * i)
                pool.wait_ge(m_ready, 2 * i + 2)
                for q in range(2):
                    pool.dma_start(gates[:, 2 * q * S:(2 * q + 2) * S].rearrange("p (k s) -> p k s", k=2),
                                   gate_fm[bass.ds(2 * i + q * KD, 2)].rearrange("k p s -> p k s")
                                   ).then_inc(gates_landed, 16)

            pool.wait_ge(unit_done, D_R)
            g.memset(sumsq[:], 0.0).then_inc(sumsq_zero, 1)
            pool.wait_ge(sumsq_zero, 1)

            def add_squares(d):
                for t in range(2):
                    pool.wait_ge(x2_squared, 2 * d + t + 1)
                    pool.wait_ge(x2_summed, 2 * d + t + 2)
                    g.tensor_tensor(sumsq[:], sumsq[:], tile(sq2, t), ALU.add).then_inc(x2_summed, 1)

            with pool.Fori(0, D_I) as i:
                for q in range(2):
                    pool.wait_ge(x2_done, 4 * i + 2 * q + 2)
                    pool.dma_start(xr[:, 2 * q * S:(2 * q + 2) * S].rearrange("p (k s) -> p k s", k=2),
                                   x_fm[bass.ds(4 * i + 2 * q, 2)].rearrange("k p s -> p k s")
                                   ).then_inc(xr_landed[q], 16)
                for q in range(2):
                    step(ADA_D + 2 * i + q, ada_acc2, q, 2 * ADA_D + 4 * i + 2 * q)
                    add_squares(2 * i + q)

            for k in range(KD):
                low(KD + k, k % 2, k, h2_full)


_INS = ["x", "c", "w_ada", "b_ada", "norm1_w", "w_in", "b_forget", "swa_q_norm_w", "swa_k_norm_w",
        "swa_sinks", "fox_q_norm_w", "fox_k_norm_w", "w_o_swa", "w_o_fox", "w_out", "norm2_w",
        "w_ffn_in", "w_ffn_out"]


def kernel(**inputs):
    import concourse.bacc as bacc
    from concourse.bass_utils import run_bass_kernel_spmd

    nc = bacc.Bacc("TRN2", target_bir_lowering=False, num_devices=1)
    arrays, args = {}, []
    for name in _INS:
        a = np.ascontiguousarray(inputs[name])
        arrays[f"in_{name}"] = a
        args.append(nc.dram_tensor(f"in_{name}", a.shape, mybir.dt.from_np(a.dtype), kind="ExternalInput").ap())
    table = shape_constants()
    arrays["in_consts"] = table
    args.append(nc.dram_tensor("in_consts", table.shape, F32, kind="ExternalInput").ap())
    args.append(nc.dram_tensor("out", (1, S, D), F32, kind="ExternalOutput").ap())
    build_block(nc, *args)
    result = run_bass_kernel_spmd(nc, [arrays], core_ids=[0])
    return result.results[0]["out"]
```

```python
from contextlib import ExitStack

import numpy as np

import concourse.bass as bass
from concourse import mybir

P = 128
ALU = mybir.AluOpType
ACT = mybir.ActivationFunctionType
F32 = mybir.dt.float32
F32R = mybir.dt.float32r

D = 2048
S = 512
TB = S // P
KD = D // P
DH = 128
HQ = 8
KVH = 2
GROUP = HQ // KVH
CHUNK = 64
DFF = ((8 * D // 3 + 255) // 256) * 256
EPS = 1e-6
NEG = -1e30
SCALE = DH ** -0.5

QA0 = 0
KA0 = HQ * DH
VA0 = KA0 + KVH * DH
QF0 = VA0 + KVH * DH
KF0 = QF0 + HQ * DH
VF0 = KF0 + HQ * DH
FL0 = VF0 + HQ * DH
G0 = FL0 + HQ
IN_TOTAL = G0 + 2 * D

UK = 4
UN = 2 * P
RING = 4
LEAD = 3
UNITS_BETWEEN = [6, 10, 13]

GK = 2
G_N = KD // GK
F_R = G_N
A_R, A_N, A_I = F_R + KD // UK, 8, HQ
B_R, B_N, B_I = A_R + A_N * A_I, 8, HQ
C_R, C_N, C_I = B_R + B_N * B_I, 4, D // UN
D_R, D_N, D_I = C_R + C_N * C_I, 8, D // UN // 2
E_R, E_N, E_I = D_R + D_N * D_I, 24, DFF // (UK * P)
STEP = KD // UK
ADA0_STEPS = 2 * D // UN
ADA_A, ADA_C = ADA0_STEPS, ADA0_STEPS + 2 * A_I
ADA_D = ADA_C + C_I
F_U = STEP * ADA0_STEPS // 2
A_U = F_U + KD // UK
B_U = A_U + 2 * A_N * A_I
C_U = B_U + B_N * B_I
D_U = C_U + 2 * C_N * C_I
E_U = D_U + 2 * D_N * D_I

CONST_W = P + 3 * S + 2 * P + HQ


def shape_constants():
    half = DH // 2
    inv = (np.float32(10000.0) ** (-np.arange(half, dtype=np.float32) / np.float32(half))).astype(np.float32)
    ang = (np.arange(S, dtype=np.float32)[:, None] * inv[None, :]).astype(np.float32)
    cos, sin = np.cos(ang).T.astype(np.float32), np.sin(ang).T.astype(np.float32)
    p = np.arange(P)[:, None]
    fox = np.where((np.arange(S)[None, :] - (S - P)) <= p, 0.0, NEG)
    j = np.arange(2 * P)[None, :]
    chunk_q, chunk_k = p // CHUNK + P // CHUNK, j // CHUNK
    swa = np.where((chunk_k == chunk_q) | (chunk_k == chunk_q - 1), 0.0, NEG)
    sel = (p % 32 == np.arange(HQ)[None, :]) * 1.0
    parts = [np.eye(P), np.concatenate([cos, cos]), np.concatenate([sin, -sin]), fox, swa, sel]
    return np.ascontiguousarray(np.concatenate(parts, axis=1).astype(np.float32))


def build_block(nc, x, c, w_ada, b_ada, norm1_w, w_in, b_forget, swa_q_norm_w, swa_k_norm_w,
                swa_sinks, fox_q_norm_w, fox_k_norm_w, w_o_swa, w_o_fox, w_out, norm2_w,
                w_ffn_in, w_ffn_out, consts, out):
    with ExitStack() as ctx:
        def sem(name):
            return ctx.enter_context(nc.semaphore(name))

        T = 4 * S
        arena_base = (nc.sbuf_base + 31) // 32 * 32
        arena_bytes = nc.sbuf_usable_end - arena_base

        def at(name, offset, cols, dt=F32):
            assert offset + 4 * cols <= arena_bytes, (name, offset, cols)
            return nc.alloc_sbuf_tensor_at(name, [P, cols], dt, offset=arena_base + offset)

        H = 0
        STORE = H + 2 * KD * T
        RAW = STORE + 36 * T
        WHI = RAW + RING * 4 * UK * UN
        WLO = WHI + RING * 4 * UK * UN
        SMALL = WLO + RING * 4 * UK * UN
        FORGET = SMALL + 2560
        TAB = FORGET + 2 * T
        WORK = TAB + 2 * T

        h_hi = at("h_hi", H, KD * S, F32R)
        h_lo = at("h_lo", H + KD * T, KD * S, F32R)
        out_rows = at("out_rows", H, TB * D)
        w_raw = at("w_raw", RAW, RING * UK * UN)
        w_hi = at("w_hi", WHI, RING * UK * UN, F32R)
        w_lo = at("w_lo", WLO, RING * UK * UN, F32R)

        shift_raw = [at(f"shift_raw{j}", (WHI, WLO)[j // 2] + (2 + j % 2) * 4 * UK * UN, UK * UN) for j in range(4)]
        x_rows = at("x_rows", STORE, TB * D)
        junk = at("junk", STORE + 16 * T, D)
        g_raw = at("g_raw", STORE + 16 * T, 2 * GK * 4 * P)
        x_raw = at("x_raw", STORE + 20 * T, KD * S)
        rot = at("rot", STORE, 10 * S)
        val = at("val", STORE + 10 * T, 10 * S)
        qf = at("qf", STORE + 20 * T, 8 * S)
        kf = at("kf", STORE + 28 * T, 8 * S)
        of_hi = at("of_hi", STORE + 20 * T, 8 * S, F32R)
        of_lo = at("of_lo", STORE + 28 * T, 8 * S, F32R)
        oa_hi = at("oa_hi", STORE + 2 * T, 8 * S, F32R)
        oa_lo = at("oa_lo", STORE + 12 * T, 8 * S, F32R)
        x2 = at("x2", STORE, KD * S)
        u_hi = at("u_hi", STORE + 16 * T, UK * S, F32R)
        u_lo = at("u_lo", STORE + 20 * T, UK * S, F32R)
        sg = at("sg", STORE + 24 * T, 2 * S)
        u_full = at("u_full", STORE + 26 * T, 2 * S)
        h2_t = at("h2_t", STORE + 28 * T, 2 * S)
        h2_full = at("h2_full", STORE + 30 * T, 2 * S)
        r2 = at("r2", STORE + 32 * T, S)
        xr = at("xr", STORE + 24 * T, 4 * S)
        sq2 = at("sq2", STORE + 28 * T, 2 * S)
        sumsq = at("sumsq", STORE + 30 * T, S)

        small_all = at("small_all", SMALL, (FORGET - SMALL) // 4)
        small, o = {}, 0
        for name, cols in (("ident", P), ("ones", P), ("mod", 6 * KD), ("bada", 6 * KD), ("vec", 64),
                           ("cact", KD), ("a1", KD), ("a2", KD), ("wy", 2), ("wx", 2), ("sinks", HQ),
                           ("sel", HQ), ("bf", 1), ("eps", 1), ("ss", TB), ("rr", TB), ("colraw", 2),
                           ("rowmax", TB), ("negmax", TB), ("rowsum", TB), ("esink", TB), ("rinv", TB),
                           ("sinkcol", 1)):
            small[name] = small_all[:, o:o + cols]
            o += cols
        assert SMALL + 4 * o <= FORGET
        ident, ones, mod, bada, vec = (small[n] for n in ("ident", "ones", "mod", "bada", "vec"))
        cact, a1, a2, wy, wx = (small[n] for n in ("cact", "a1", "a2", "wy", "wx"))
        sinks, sel, bf, eps, ss, rr = (small[n] for n in ("sinks", "sel", "bf", "eps", "ss", "rr"))
        colraw, rowmax, negmax, rowsum = (small[n] for n in ("colraw", "rowmax", "negmax", "rowsum"))
        esink, rinv, sinkcol = (small[n] for n in ("esink", "rinv", "sinkcol"))
        fq_rows = at("fq_rows", FORGET, S, F32R)
        fk_rows = at("fk_rows", FORGET + T, S, F32R)
        cos = at("cos", TAB, S)
        sin = at("sin", TAB + T, S)
        foxmask = at("foxmask", TAB, S)
        swamask = at("swamask", TAB + T, 2 * P)
        ada_acc = at("ada_acc", WORK, 4 * UN)
        ada_acc2 = at("ada_acc2", FORGET, 4 * UN)
        ada_sum = at("ada_sum", WORK + 16 * UN, UN)
        W4 = WORK + 20 * UN
        full = at("full", W4, 4 * S)
        sq = at("sq", W4, 2 * S)
        rs = at("rs", W4 + 2 * T, 2 * S)
        vecrows = at("vecrows", W4, 2 * P)
        diag = at("diag", W4 + 2 * T, S)
        BW = TAB + T + 8 * P
        logits = at("logits", BW, 10 * P)
        pt = at("pt", BW + 40 * P, 10 * P)
        v_head = at("v_head", BW, S)
        gst = at("gst", BW + 80 * P, 2 * S)
        q_fox = at("q_fox", BW + 40 * P, S)
        fq_head = at("fq_head", BW + 40 * P + T, S, F32R)
        q_swa = at("q_swa", BW + 80 * P + T, S)
        gates = at("gates", W4, 4 * S)
        fz = at("fz", FORGET, 2 * S)

        bank = [ctx.enter_context(nc.psum_tensor(f"bank{b}", [P, S], F32)) for b in range(8)]

        x_fm = nc.dram_tensor("x_fm", [KD, P, S], F32).ap()
        gate_fm = nc.dram_tensor("gate_fm", [2 * KD, P, S], F32).ap()

        raw_landed = [sem(f"raw_landed{s}") for s in range(RING)]
        hi_done, lo_done, unit_done = sem("hi_done"), sem("lo_done"), sem("unit_done")
        ada_mac, ada_summed, ada_cols = sem("ada_mac"), sem("ada_summed"), sem("ada_cols")
        col_copied, mod_ready, scale_ready = sem("col_copied"), sem("mod_ready"), sem("scale_ready")
        const_landed, vec_landed = sem("const_landed"), sem("vec_landed")
        x_landed = [sem(f"x_landed{t}") for t in range(TB)]
        ones_set, vecs_turned, vecs_copied, cact_done = (
            sem("ones_set"), sem("vecs_turned"), sem("vecs_copied"), sem("cact_done"))
        shift_landed = [sem(f"shift_landed{j}") for j in range(4)]
        weights_ready = sem("weights_ready")
        g_landed = [sem("g_landed0"), sem("g_landed1")]
        x_squared, r_root, r_ready, diag_ready = (
            sem("x_squared"), sem("r_root"), sem("r_ready"), sem("diag_ready"))
        x_turned, xt_copied, x_spilled, xn_ready = (
            sem("x_turned"), sem("xt_copied"), sem("x_spilled"), sem("xn_ready"))
        h_full, h_hi_done, h_ready = sem("h_full"), sem("h_hi_done"), sem("h_ready")
        act_evicted = sem("act_evicted")
        tab_landed, vec_zeroed, y_rooted, x_rooted = sem("tab_landed"), sem("vec_zeroed"), sem("y_rooted"), sem("x_rooted")
        sink_set, sumsq_zero, a1_step = sem("sink_set"), sem("sumsq_zero"), sem("a1_step")
        f_act, f_dve, rows_zeroed = sem("f_act"), sem("f_dve"), sem("rows_zeroed")
        y_posts, y_stats, y_chain = sem("y_posts"), sem("y_stats"), sem("y_chain")
        x_posts, x_stats, x_chain = sem("x_posts"), sem("x_stats"), sem("x_chain")
        masks_landed = sem("masks_landed")
        q_copied, fq_done = sem("q_copied"), sem("fq_done")
        s_done, s_stats, negmax_done, p_done, sums_added, rinv_done = (
            sem("s_done"), sem("s_stats"), sem("negmax_done"), sem("p_done"), sem("sums_added"), sem("rinv_done"))
        p_scaled, p_turned, pt_act, pt_dve, v_copied, pv_done, o_hi_done, o_ready = (
            sem("p_scaled"), sem("p_turned"), sem("pt_act"), sem("pt_dve"), sem("v_copied"),
            sem("pv_done"), sem("o_hi_done"), sem("o_ready"))
        gate_spilled, gates_landed = sem("gate_spilled"), sem("gates_landed")
        m_step, m_hi_done, m_ready = sem("m_step"), sem("m_hi_done"), sem("m_ready")
        xr_landed = [sem("xr_landed0"), sem("xr_landed1")]
        x2_done, x2_squared, x2_summed = sem("x2_done"), sem("x2_squared"), sem("x2_summed")
        r2_sum, r2_root, r2_ready, h2_scaled = sem("r2_sum"), sem("r2_root"), sem("r2_ready"), sem("h2_scaled")
        u_mul, u_hi_done, u_ready = sem("u_mul"), sem("u_hi_done"), sem("u_ready")
        acc_done = sem("acc_done")
        o_block_turned, out_copied_a, out_copied_d, out_stored = (
            sem("o_block_turned"), sem("out_copied_a"), sem("out_copied_d"), sem("out_stored"))

        w_in_k = w_in[0].rearrange("(t p) n -> p t n", p=P)
        w_ada_k = w_ada[0].rearrange("(t p) n -> p t n", p=P)
        w_oa_k = w_o_swa[0].rearrange("(t p) n -> p t n", p=P)
        w_of_k = w_o_fox[0].rearrange("(t p) n -> p t n", p=P)
        w_out_k = w_out[0].rearrange("(t p) n -> p t n", p=P)
        w_fi_k = w_ffn_in[0].rearrange("(t p) n -> p t n", p=P)
        w_fo_k = w_ffn_out[0].rearrange("(t p) n -> p t n", p=P)
        x_tb = x[0].rearrange("(t p) n -> t p n", p=P)
        out_tb = out[0].rearrange("(t p) n -> t p n", p=P)

        def tile(t, n, width=S):
            if isinstance(n, int):
                return t[:, n * width:(n + 1) * width]
            return t[:, bass.ds(n * width, width)]

        def col(t, n, k=1):
            return t[:, n:n + k] if isinstance(n, int) else t[:, bass.ds(n, k)]

        def unit(t, u):
            return t[:, (u % RING) * UK * UN:(u % RING + 1) * UK * UN]


        ph_f = dict(r=F_R, n=4, it=1, u=F_U, ada=None)
        ph_a = dict(r=A_R, n=A_N, it=A_I, u=A_U, ada=ADA_A)
        ph_b = dict(r=B_R, n=B_N, it=B_I, u=B_U, ada=None)
        ph_c = dict(r=C_R, n=C_N, it=C_I, u=C_U, ada=ADA_C)
        ph_d = dict(r=D_R, n=D_N, it=D_I, u=D_U, ada=ADA_D)
        ph_e = dict(r=E_R, n=E_N, it=E_I, u=E_U, ada=None)
        after = {id(a): b for a, b in zip((ph_f, ph_a, ph_b, ph_c, ph_d),
                                          (ph_a, ph_b, ph_c, ph_d, ph_e))}

        def ahead(ph, i, j, last):
            j += LEAD
            if j < ph["n"]:
                return ph, i, j
            if not last:
                return ph, i + 1, j - ph["n"]
            if ph is ph_e:
                return None
            return after[id(ph)], 0, j - ph["n"]

        def numbers(ph, i, j):
            k = 2 if ph["ada"] is not None else 1
            u = ph["u"] + k * j
            return ph["r"] + ph["n"] * i + j, u % RING, u // RING + i * (k * ph["n"] // RING)

        def each(eng, n, body, start=0):
            if n - start > 1:
                with eng.Fori(start, n - 1) as i:
                    body(i, False)
            body(n - 1, True)

        def y_rotate(eng, y):
            hd, tmp = tile(rs, 0), tile(rs, 1)
            n = 6 * y
            half = DH // 2
            eng.wait_ge(y_chain, n + 1)
            eng.tensor_tensor(hd, tile(rot, y), hd, ALU.mult).then_inc(y_chain, 1)
            eng.wait_ge(y_chain, n + 2)
            eng.tensor_tensor(tmp[0:half], hd[half:DH], sin[half:DH, :], ALU.mult).then_inc(y_chain, 1)
            eng.tensor_tensor(tmp[half:DH], hd[0:half], sin[0:half, :], ALU.mult).then_inc(y_chain, 1)
            eng.wait_ge(y_chain, n + 4)
            eng.tensor_tensor(hd, hd, cos[:], ALU.mult).then_inc(y_chain, 1)
            eng.wait_ge(y_chain, n + 5)
            dst = tile(rot, y) if isinstance(y, int) else rot[:, bass.ds((y - 1) * S + S, S)]
            eng.tensor_tensor(dst, hd, tmp, ALU.add).then_inc(y_chain, 1)

        fox_blocks = [list(range(qb + 1)) for qb in range(TB)]
        swa_blocks = [list(range(max(qb - 1, 0), qb + 1)) for qb in range(TB)]

        def starts(blocks):
            n, got = 0, []
            for b in blocks:
                got.append(n)
                n += len(b)
            return got

        fox_at = [(4 + qb, 0) for qb in range(TB)]
        swa_at = [(6, 0), (6, P), (7, 0), (7, 2 * P)]
        fox_pt = [(7, n) for n in range(4)] + [(5, n) for n in range(3)] + [(6, n) for n in range(3)]
        swa_pt = [(7, n) for n in range(4)] + [(6, n) for n in range(3)]

        block = ctx.enter_context(nc.Block())

        @block.sync
        def _(sp):
            sp.dma_start(ident[:], consts[:, 0:P]).then_inc(const_landed, 16)

            def load_x(tb):
                sp.dma_start(x_rows[:, tb * D:(tb + 1) * D], x_tb[tb]).then_inc(x_landed[tb], 16)

            def load(u, src, width=UN):
                dst = unit(w_raw, u).rearrange("p (k n) -> p k n", k=UK)
                sp.dma_start(dst[:, :, 0:width], src).then_inc(raw_landed[u % RING], 32)

            def load_pair(u, kq, col0, col1):
                dst = unit(w_raw, u).rearrange("p (k n) -> p k n", k=UK)
                for t, c0 in enumerate((col0, col1)):
                    sp.dma_start(dst[:, :, t * P:(t + 1) * P],
                                 w_in_k[:, kq * UK:(kq + 1) * UK, bass.ds(c0, P)]).then_inc(raw_landed[u % RING], 16)

            def load_ada(u, kq, c0):
                load(u, w_ada_k[:, kq * UK:(kq + 1) * UK, bass.ds(c0, UN)])

            def load_shift(j, c0):
                sp.dma_start(shift_raw[j][:].rearrange("p (k n) -> p k n", k=UK),
                             w_ada_k[:, j * UK:(j + 1) * UK, bass.ds(c0, UN)]).then_inc(shift_landed[j], 16)

            def split(r):
                sp.wait_ge(lo_done, r + 1)

            def summed(a):
                sp.wait_ge(ada_mac, UK * (a + 1))

            load_ada(0, 0, D)
            load_ada(1, 1, D)
            sp.wait_ge(vec_zeroed, 1)
            rows = [(c, 0), (norm1_w, KD), (norm2_w, 2 * KD)]
            for v, r0 in rows:
                sp.dma_start(vecrows[r0:r0 + KD, 0:P], v.rearrange("a (r p) -> (a r) p", p=P)).then_inc(vec_landed, 16)
            for n, w in enumerate((swa_q_norm_w, swa_k_norm_w, fox_q_norm_w, fox_k_norm_w)):
                sp.dma_start(vecrows[3 * KD + n:3 * KD + n + 1, 0:P], w).then_inc(vec_landed, 16)
            sp.dma_start(vecrows[0:6 * KD, P:2 * P], b_ada.rearrange("a (r p) -> (a r) p", p=P)).then_inc(vec_landed, 16)
            load_x(0)
            load_ada(2, 2, D)
            load_x(1)
            load_ada(3, 3, D)
            load_x(2)
            load_x(3)

            def load_first(p, slot):
                k0 = p * GK
                rows = w_in_k[:, k0:k0 + GK, KA0:KA0 + 4 * P] if isinstance(p, int) else \
                    w_in_k[:, bass.ds(k0, GK), KA0:KA0 + 4 * P]
                sp.dma_start(g_raw[:, slot * GK * 4 * P:(slot + 1) * GK * 4 * P].rearrange("p (k n) -> p k n", k=GK),
                             rows).then_inc(g_landed[slot], 16)

            for j in range(STEP):
                load_shift(j, 0)
            sp.wait_ge(x_squared, TB)
            load_first(0, 0)
            load_first(1, 1)

            def pairs(i, last):
                for q in range(4):
                    p = 4 * i + q
                    if last and q == 3:
                        break
                    for j in range(STEP):
                        summed(2 * STEP * p + j)
                        load_ada(j, j, (p + 1) * UN + D)
                    for j in range(STEP):
                        summed(2 * STEP * p + STEP + j)
                        load_shift(j, (p + 1) * UN)
                    if not (last and q >= 2):
                        split(p)
                        load_first(p + 2, q % 2)
            each(sp, ADA0_STEPS // 8, pairs)

            for kq in range(4):
                summed(STEP * (ADA0_STEPS - 2) + kq)
                load(F_U + kq, w_in_k[:, kq * UK:(kq + 1) * UK, FL0:FL0 + P], width=P)
            sp.dma_start(cos[:], consts[:, P:P + S]).then_inc(tab_landed, 16)
            sp.dma_start(sin[:], consts[:, P + S:P + 2 * S]).then_inc(tab_landed, 16)
            sp.dma_start(sel[:], consts[:, CONST_W - HQ:CONST_W]).then_inc(tab_landed, 16)
            sp.dma_start(sinks[:], swa_sinks.to_broadcast([P, HQ])).then_inc(tab_landed, 16)
            sp.dma_start(bf[0:HQ, :], b_forget.rearrange("a h -> h a")).then_inc(tab_landed, 16)

            with sp.Fori(0, A_I) as i:
                for j in range(A_N):
                    split(A_R + A_N * i + j - 2)
                    if j < 4:
                        load_pair(A_U + 2 * j, j, (i + QF0 // P) * P, (i + KF0 // P) * P)
                    else:
                        load_pair(A_U + 2 * j, j - 4, QA0 + i * P, VF0 + i * P)
                    summed(STEP * ADA_A + A_N * i + j - 2)
                    load_ada(A_U + 2 * j + 1, j % STEP, (2 * ADA_A + j // STEP * 2) * P + i * 2 * UN)

            summed(STEP * ADA_C - 1)
            split(B_R - 1)
            with sp.Fori(0, B_I) as i:
                for j in range(B_N):
                    split(B_R + B_N * i + j - RING)
                    load(B_U + j, w_in_k[:, (j % 4) * UK:(j % 4 + 1) * UK, bass.ds(G0 + (j // 4) * D + i * UN, UN)])

            split(C_R - 1)
            with sp.Fori(0, C_I) as i:
                for j in range(C_N):
                    split(C_R + C_N * i + j - 2)
                    w = (w_oa_k, w_of_k)[j // 2]
                    load(C_U + 2 * j, w[:, (j % 2) * UK:(j % 2 + 1) * UK, bass.ds(i * UN, UN)])
                    summed(STEP * ADA_C + C_N * i + j - 2)
                    load_ada(C_U + 2 * j + 1, j, 2 * ADA_C * P + i * UN)

            with sp.Fori(0, D_I) as i:
                for j in range(D_N):
                    split(D_R + D_N * i + j - 2)
                    load(D_U + 2 * j, w_out_k[:, (j % 4) * UK:(j % 4 + 1) * UK, bass.ds((j // 4) * UN + i * 2 * UN, UN)])
                    summed(STEP * ADA_D + D_N * i + j - 2)
                    load_ada(D_U + 2 * j + 1, j % STEP, (2 * ADA_D + j // STEP * 2) * P + i * 2 * UN)

            summed(STEP * (ADA_D + 2 * D_I) - 1)
            split(E_R - 1)
            with sp.Fori(0, E_I) as i:
                for j in range(E_N):
                    split(E_R + E_N * i + j - RING)
                    if j < 16:
                        pair, kq = j // 4, j % 4
                        c0 = (pair % 2) * DFF + (pair // 2) * UN
                        load(E_U + j, w_fi_k[:, kq * UK:(kq + 1) * UK, bass.ds(c0 + i * UK * P, UN)])
                    else:
                        load(E_U + j, w_fo_k[:, bass.ds(i * UK, UK), (j - 16) * UN:(j - 15) * UN])

            for m in range(TB * TB):
                tb, n4 = m % TB, m // TB
                sp.wait_ge((out_copied_a, out_copied_d)[m % 2], m // 2 + 1)
                sp.dma_start(out_tb[tb][:, n4 * S:(n4 + 1) * S],
                             out_rows[:, tb * D + n4 * S:tb * D + (n4 + 1) * S]).then_inc(out_stored, 16)
            sp.wait_ge(out_stored, 16 * TB * TB)

        @block.tensor
        def _(pe):
            def gemm(r, slot, hi, lo, k0, banks, first, last, ready=None, reads=None, ks=range(UK)):
                if ks[0] == 0:
                    pe.wait_ge(lo_done, r + 1)
                whi, wlo = unit(w_hi, slot), unit(w_lo, slot)
                for k in ks:
                    if ready is not None:
                        pe.wait_ge(ready, reads(k0 + k))
                    for t, b in enumerate(banks):
                        cols = slice(k * UN + t * P, k * UN + (t + 1) * P)
                        first_k, last_k = first and k == 0, last and k == UK - 1
                        xh, xl = tile(hi, k0 + k), tile(lo, k0 + k)
                        nc.tensor.matmul(bank[b][:], lhsT=whi[:, cols], rhs=xh, start=first_k, stop=False)
                        nc.tensor.matmul(bank[b][:], lhsT=whi[:, cols], rhs=xl, start=False, stop=False)
                        mm = nc.tensor.matmul(bank[b][:], lhsT=wlo[:, cols], rhs=xh, start=False, stop=last_k)
                if ks[-1] == UK - 1:
                    mm.then_inc(unit_done, 1)

            def cols_of_step(s):
                pe.wait_ge(ada_summed, s + 3)
                pe.wait_ge(col_copied, s + 1)
                for t in range(2):
                    mm = nc.tensor.matmul(bank[4][:, t:t + 1], lhsT=ada_sum[:, t * P:(t + 1) * P],
                                          rhs=ones[:, 0:1], start=True, stop=True)
                mm.then_inc(ada_cols, 1)

            pe.wait_ge(const_landed, 16)
            pe.wait_ge(ones_set, 1)
            pe.wait_ge(vec_landed, 16 * 8)
            nc.tensor.transpose(bank[5][:, 0:P], vecrows[:, 0:P], ident[:])
            nc.tensor.transpose(bank[5][:, P:2 * P], vecrows[:, P:2 * P], ident[:]).then_inc(vecs_turned, 1)
            for tb in range(TB):
                pe.wait_ge(x_landed[tb], 16)
            for k in range(KD):
                if k >= 4:
                    pe.wait_ge(xt_copied, k - 3)
                for tb in range(TB):
                    mm = nc.tensor.transpose(bank[k % 4][:, tb * P:(tb + 1) * P],
                                             x_rows[:, tb * D + k * P:tb * D + (k + 1) * P], ident[:])
                mm.then_inc(x_turned, 1)

            def normalised(p):
                if p:
                    pe.wait_ge(h_full, 2 * p)
                for t in range(2):
                    k = 2 * p + t
                    for tb in range(TB):
                        mm = nc.tensor.matmul(bank[5 + t][:, tb * P:(tb + 1) * P],
                                              lhsT=x_rows[:, tb * D + k * P:tb * D + (k + 1) * P],
                                              rhs=diag[:, tb * P:(tb + 1) * P], start=True, stop=True)
                mm.then_inc(xn_ready, 1)

            def first_unit(p, kk):
                if kk == 0:
                    pe.wait_ge(lo_done, p + 1)
                k = GK * p + kk
                pe.wait_ge(h_ready, k + 3)
                whi, wlo = unit(w_hi, p % 2), unit(w_lo, p % 2)
                xh, xl = tile(h_hi, k), tile(h_lo, k)
                for t, b in enumerate((2, 0, 3, 1)):
                    cols = slice((kk * 4 + t) * P, (kk * 4 + t + 1) * P)
                    nc.tensor.matmul(bank[b][:], lhsT=whi[:, cols], rhs=xh, start=k == 0, stop=False)
                    nc.tensor.matmul(bank[b][:], lhsT=whi[:, cols], rhs=xl, start=False, stop=False)
                    mm = nc.tensor.matmul(bank[b][:], lhsT=wlo[:, cols], rhs=xh, start=False, stop=k == KD - 1)
                if kk == GK - 1:
                    mm.then_inc(unit_done, 1)

            pe.wait_ge(xt_copied, KD)
            pe.wait_ge(vecs_copied, 2)
            pe.wait_ge(diag_ready, TB)
            normalised(0)
            cols_of_step(0)
            for p in range(G_N):
                cols_of_step(2 * p + 1)
                if p:
                    first_unit(p - 1, 1)
                first_unit(p, 0)
                if p < G_N - 1:
                    cols_of_step(2 * p + 2)
                    normalised(p + 1)
            first_unit(G_N - 1, 1)

            def y_post(y, evicted):
                pe.wait_ge(act_evicted, evicted)
                pe.wait_ge(y_stats, y + 1)
                nc.tensor.matmul(bank[6][:], lhsT=ones[:], rhs=tile(sq, 0), start=True, stop=True)
                for tb in range(TB):
                    mm = nc.tensor.transpose(bank[7][:, tb * P:(tb + 1) * P],
                                             sq[:, S + tb * P:S + (tb + 1) * P], ident[:])
                mm.then_inc(y_posts, 1)

            for j in range(4):
                gemm(F_R + j, F_R + j, h_hi, h_lo, UK * j, (5,), j == 0, j == 3)
                if j == 0:
                    y_post(0, 1)

            with pe.Fori(0, A_I) as i:
                for j in range(A_N):
                    if j == 0:
                        pe.wait_ge(act_evicted, 2 * i + 2)
                    if j == 4:
                        pe.wait_ge(act_evicted, 2 * i + 3)
                    gemm(A_R + A_N * i + j, A_R + j, h_hi, h_lo, UK * (j % 4),
                         ((2, 3), (0, 1))[j // 4], j % 4 == 0, j % 4 == 3)
                    if j == 0:
                        y_post(i + 1, 2 * i + 3)
                    if j == 2:
                        cols_of_step(ADA_A + 2 * i)
                    if j == 4:
                        pe.wait_ge(act_evicted, 2 * i + 4)
                        pe.wait_ge(col_copied, ADA_A + 2 * i + 2)
                        for t in range(2):
                            mm = nc.tensor.matmul(bank[4 + t][:], lhsT=ones[:], rhs=tile(sq, t),
                                                  start=True, stop=True)
                        mm.then_inc(x_posts, 1)
                    if j == 6:
                        pe.wait_ge(x_stats, i + 1)
                        cols_of_step(ADA_A + 2 * i + 1)
            y_post(KVH + HQ - 1, 2 * HQ + 3)

            def probabilities(where, n):
                pe.wait_ge(p_scaled, n)
                for b, (bk, cb) in enumerate(where):
                    mm = nc.tensor.transpose(bank[bk][:, cb * P:(cb + 1) * P], logits[:, b * P:(b + 1) * P], ident[:])
                mm.then_inc(p_turned, 1)

            def weighted_values(blocks, n):
                pe.wait_ge(pt_act, n)
                pe.wait_ge(pt_dve, n)
                pe.wait_ge(v_copied, n)
                pe.wait_ge(o_ready, n + 1)
                for qb, b0 in enumerate(starts(blocks)):
                    for m, kb in enumerate(blocks[qb]):
                        mm = nc.tensor.matmul(bank[4][:, qb * P:(qb + 1) * P], lhsT=v_head[:, kb * P:(kb + 1) * P],
                                              rhs=pt[:, (b0 + m) * P:(b0 + m + 1) * P],
                                              start=m == 0, stop=m == len(blocks[qb]) - 1)
                mm.then_inc(pv_done, 1)

            with pe.Fori(0, B_I) as h:
                for j in range(B_N):
                    if j == 0:
                        pe.wait_ge(act_evicted, 2 * h + 18)
                    if j == 4:
                        pe.wait_ge(act_evicted, 2 * h + 19)
                    gemm(B_R + B_N * h + j, B_R + j, h_hi, h_lo, UK * (j % 4),
                         ((2, 3), (0, 1))[j // 4], j % 4 == 0, j % 4 == 3)
                    if j == 0:
                        pe.wait_ge(q_copied, 2 * h + 1)
                        pe.wait_ge(fq_done, h + 1)
                        pe.wait_ge(o_ready, 2 * h + 2)
                        pe.wait_ge(y_stats, KVH + HQ + 1)
                        pe.wait_ge(col_copied, ADA_C + 1)
                        for qb in range(TB):
                            n = (qb + 1) * P
                            nc.tensor.matmul(bank[4 + qb][:, 0:n], lhsT=q_fox[:, qb * P:(qb + 1) * P],
                                             rhs=kf[:, bass.ds(h * S, n)], start=True, stop=False)
                            mm = nc.tensor.matmul(bank[4 + qb][:, 0:n], lhsT=fq_head[:, qb * P:(qb + 1) * P],
                                                  rhs=fk_rows[:, 0:n], start=False, stop=True)
                        mm.then_inc(s_done, 1)
                    if j == 2:
                        probabilities(fox_pt, 2 * h + 1)
                    if j == 3:
                        weighted_values(fox_blocks, 2 * h + 1)
                        pe.wait_ge(q_copied, 2 * h + 2)
                        for qb in range(TB):
                            bk, c0 = swa_at[qb]
                            kb = swa_blocks[qb]
                            mm = nc.tensor.matmul(bank[bk][:, c0:c0 + len(kb) * P],
                                                  lhsT=q_swa[:, qb * P:(qb + 1) * P],
                                                  rhs=rot[:, bass.ds((h // GROUP) * S + kb[0] * P, len(kb) * P)],
                                                  start=True, stop=True)
                        mm.then_inc(s_done, 1)
                    if j == 5:
                        probabilities(swa_pt, 2 * h + 2)
                    if j == 6:
                        weighted_values(swa_blocks, 2 * h + 2)

            pe.wait_ge(act_evicted, 34)
            with pe.Fori(0, C_I) as i:
                pe.wait_ge(o_ready, 2 * HQ + 2)
                for j in range(C_N):
                    if j == 0:
                        pe.wait_ge(m_step, 6 * i + 2)
                    if j == 2:
                        pe.wait_ge(act_evicted, 35)
                        pe.wait_ge(m_step, 6 * i + 4)
                    hi, lo = ((oa_hi, oa_lo), (of_hi, of_lo))[j // 2]
                    gemm(C_R + C_N * i + j, C_R + j, hi, lo, UK * (j % 2),
                         ((2, 3), (0, 1))[j // 2], j % 2 == 0, j % 2 == 1)
                    if j == 2:
                        cols_of_step(ADA_C + i)

            with pe.Fori(0, D_I) as i:
                for j in range(D_N):
                    if j % 4 == 0:
                        pe.wait_ge(m_step, 6 * C_I + 2 + j // 2)
                        pe.wait_ge(x2_done, 4 * i + j // 2 + 2)
                    gemm(D_R + D_N * i + j, D_R + j, h_hi, h_lo, UK * (j % 4),
                         ((2, 3), (0, 1))[j // 4], j % 4 == 0, j % 4 == 3,
                         m_ready if j < 4 else None, lambda k: k + 3)
                    if j in (2, 6):
                        cols_of_step(ADA_D + 2 * i + j // 4)
            pe.wait_ge(x2_summed, KD)
            pe.wait_ge(col_copied, ADA_D + 2 * D_I + 1)
            nc.tensor.matmul(bank[4][:], lhsT=ones[:], rhs=sumsq[:], start=True, stop=False)
            for t in range(2):
                pe.wait_ge(x2_squared, KD - 1 + t)
                mm = nc.tensor.matmul(bank[4][:], lhsT=ones[:], rhs=tile(sq2, t), start=False, stop=t == 1)
            mm.then_inc(r2_sum, 1)

            def ffn_banks(q):
                return (((2, 3), (0, 1))[q % 2] if q < 4 else ((4, 5), (6, 7), (2, 3), (0, 1))[q % 4])

            with pe.Fori(0, E_I) as i:
                waits = [(acc_done, 7, 8), (acc_done, 8, 8), (act_evicted, 36, 2), (u_mul, 2, 4),
                         (acc_done, 5, 8), (acc_done, 6, 8), (act_evicted, 37, 2), (u_mul, 4, 4)] + [
                         (acc_done, 9 + n, 8) for n in range(4)]

                def banks_free(q):
                    s0, n0, step0 = waits[q]
                    pe.wait_ge(s0, i * step0 + n0)
                    return ffn_banks(q)

                for q in range(4):
                    banks = banks_free(q)
                    for j in range(4 * q, 4 * q + 4):
                        gemm(E_R + E_N * i + j, E_R + j, h_hi, h_lo, UK * (j % 4), banks, j % 4 == 0,
                             j % 4 == 3, h_ready if q == 0 else None, lambda k: KD + k + 3)
                for ks in ((0, 1), (2, 3)):
                    for q in (4, 5):
                        j = 12 + q
                        banks = banks_free(q) if ks[0] == 0 else ffn_banks(q)
                        gemm(E_R + E_N * i + j, E_R + j, u_hi, u_lo, 0, banks, True, True, u_ready,
                             lambda k: i * UK + k + 1, ks)
                for q in range(6, 12):
                    j = 12 + q
                    gemm(E_R + E_N * i + j, E_R + j, u_hi, u_lo, 0, banks_free(q), True, True)

            for m in range(TB * TB):
                n4, tb = m // TB, m % TB
                if tb == 0:
                    pe.wait_ge(acc_done, 8 * E_I + (6 if n4 == 0 else 8))
                if m >= 8:
                    pe.wait_ge((out_copied_a, out_copied_d)[m % 2], (m - 8) // 2 + 1)
                for q in range(TB):
                    f0 = (n4 * TB + q) * S + tb * P
                    mm = nc.tensor.transpose(bank[(m + 4) % 8][:, q * P:(q + 1) * P], x2[:, f0:f0 + P], ident[:])
                mm.then_inc(o_block_turned, 1)

        @block.scalar
        def _(act):
            def split(ph, i, j, last):
                at_ = ahead(ph, i, j, last)
                if at_ is None:
                    return
                r, slot, use = numbers(*at_)
                act.wait_ge(raw_landed[slot], use * 32 + 32)
                if at_[0] is ph_f:
                    act.wait_ge(unit_done, min(r - 1, G_N))
                    act.wait_ge(ada_mac, UK * STEP * ADA0_STEPS)
                else:
                    act.wait_ge(unit_done, r - RING + 1)
                ws = numbers(at_[0], 0, at_[2])[0] % RING
                n = P if at_[0] is ph_f else UN
                view = [unit(t, s).rearrange("p (k n) -> p k n", k=UK)[:, :, 0:n]
                        for t, s in ((w_raw, slot), (w_hi, ws))]
                nc.scalar.activation(view[1], view[0], ACT.Copy).then_inc(hi_done, 1)

            def copy_cols(s):
                act.wait_ge(ada_cols, s + 2)
                act.wait_ge(mod_ready, s + 1)
                nc.scalar.activation(colraw[:], bank[4][:, 0:2], ACT.Copy).then_inc(col_copied, 1)

            act.wait_ge(vecs_copied, 1)
            nc.scalar.activation(cact[:], vec[:, 0:KD], ACT.Silu).then_inc(cact_done, 1)
            for tb in range(TB):
                act.wait_ge(x_landed[tb], 16)
                if tb:
                    act.wait_ge(x_squared, tb)
                nc.scalar.activation(junk[:], x_rows[:, tb * D:(tb + 1) * D], ACT.Square,
                                     accum_out=ss[:, tb:tb + 1]).then_inc(x_squared, 1)
            act.wait_ge(x_squared, TB)
            nc.scalar.activation(rr[:], ss[:], ACT.Sqrt, bias=eps[:], scale=1.0 / D).then_inc(r_root, 1)
            for k in range(KD):
                act.wait_ge(x_turned, k + 1)
                nc.scalar.activation(tile(x_raw, k), bank[k % 4][:], ACT.Copy).then_inc(xt_copied, 1)

            def h_tile(n, k, t, src, a, b, whole):
                act.wait_ge(h_ready, n + 1)
                nc.scalar.activation(tile(whole, t), src, ACT.Identity, scale=a, bias=b).then_inc(h_full, 1)
                act.wait_ge(h_full, n + 1)
                nc.scalar.activation(tile(h_hi, k), tile(whole, t), ACT.Copy).then_inc(h_hi_done, 1)

            with act.Fori(0, G_N // 4) as i:
                for q in range(4):
                    p = 4 * i + q
                    copy_cols(2 * p)
                    act.wait_ge(g_landed[q % 2], 32 * i + 16 * (q // 2) + 16)
                    nc.scalar.activation(unit(w_hi, q % 2), g_raw[:, (q % 2) * UK * UN:(q % 2 + 1) * UK * UN],
                                         ACT.Copy).then_inc(hi_done, 1)
                    copy_cols(2 * p + 1)
                    act.wait_ge(xn_ready, p + 1)
                    act.wait_ge(mod_ready, 2 * p + 3)
                    act.wait_ge(scale_ready, p + 1)
                    for t in range(2):
                        h_tile(2 * p + t, 2 * p + t, t, bank[5 + t][:], col(a1, 2 * p + t), col(mod, 2 * p + t), full)

            def y_evict(y, b):
                nc.scalar.activation(tile(sq, 0), bank[b][:], ACT.Square)
                w = 0 if isinstance(y, int) and y < KVH else 1
                nc.scalar.activation(tile(rot, y), bank[b][:], ACT.Identity, scale=wy[:, w:w + 1])
                nc.scalar.activation(tile(sq, 1), bank[b + 1][:], ACT.Copy).then_inc(act_evicted, 1)

            def y_roots(y):
                act.wait_ge(y_posts, y + 1)
                nc.scalar.activation(tile(rs, 0), bank[6][:], ACT.Sqrt, bias=eps[:], scale=1.0 / DH).then_inc(y_rooted, 1)
                nc.scalar.activation(tile(val, y), bank[7][:], ACT.Copy).then_inc(y_stats, 1)

            for k in range(0, KD, 4):
                act.dma_start(x_fm[k:k + 4].rearrange("k p s -> p k s"),
                              x_raw[:, k * S:(k + 4) * S].rearrange("p (k s) -> p k s", k=4)
                              ).then_inc(x_spilled, 16)
            for j in range(LEAD):
                split(ph_f, 0, j - LEAD, False)
            act.wait_ge(weights_ready, 1)
            act.wait_ge(unit_done, G_N)
            y_evict(0, 2)
            for j in range(4):
                split(ph_f, 0, j, True)
                if j == 1:
                    y_roots(0)
                    y_evict(1, 0)
            act.wait_ge(unit_done, F_R + 4)
            act.wait_ge(tab_landed, 16 * 5)
            act.wait_ge(f_dve, 1)
            nc.scalar.activation(fz[0:HQ, S:2 * S], bank[5][0:HQ, :], ACT.Identity, bias=bf[0:HQ, :]).then_inc(act_evicted, 1)

            def forget():
                for n, (f, b) in enumerate(((ACT.Exp, 0.0), (ACT.Ln, ones[0:HQ, 0:1]))):
                    act.wait_ge((f_dve, f_act)[n], 2 - n)
                    nc.scalar.activation(fz[0:HQ, 0:S], fz[0:HQ, 0:S], f, bias=b).then_inc(f_act, 1)

            def heads(i, last):
                for j in range(A_N):
                    split(ph_a, i, j, last)
                    if j == 1:
                        act.wait_ge(x_chain, 4 * i + 4)
                        act.wait_ge(y_chain, 6 * i + 6)
                        y_roots(i + 1)
                    if j == 3:
                        copy_cols(ADA_A + 2 * i)
                    if j == 4:
                        act.wait_ge(x_spilled, 16 * 4)
                        act.wait_ge(unit_done, A_R + A_N * i + 4)
                        nc.scalar.activation(tile(sq, 0), bank[2][:], ACT.Square)
                        nc.scalar.activation(tile(sq, 1), bank[3][:], ACT.Square)
                        nc.scalar.activation(tile(qf, i), bank[2][:], ACT.Identity, scale=wx[:, 0:1])
                        nc.scalar.activation(tile(kf, i), bank[3][:], ACT.Identity,
                                             scale=wx[:, 1:2]).then_inc(act_evicted, 1)
                    if j == 5:
                        act.wait_ge(x_posts, i + 1)
                        act.wait_ge(y_chain, 6 * i + 12)
                        for t in range(2):
                            nc.scalar.activation(tile(rs, t), bank[4 + t][:], ACT.Sqrt, bias=eps[:],
                                                 scale=1.0 / DH).then_inc(x_stats if t else x_rooted, 1)
                    if j == 3 and last:
                        forget()
                    if j == 7:
                        copy_cols(ADA_A + 2 * i + 1)
                act.wait_ge(unit_done, A_R + A_N * i + 8)
                y_evict(i + KVH, 0)
            each(act, A_I, heads)
            act.wait_ge(x_chain, 4 * A_I + 4)
            act.wait_ge(y_chain, 6 * (KVH + HQ - 1))
            y_roots(KVH + HQ - 1)

            def exponentials(blocks, n, h=None):
                act.wait_ge(negmax_done, n)
                for qb, b0 in enumerate(starts(blocks)):
                    w = slice(b0 * P, (b0 + len(blocks[qb])) * P)
                    ex = nc.scalar.activation(logits[:, w], logits[:, w], ACT.Exp, bias=negmax[:, qb:qb + 1],
                                              accum_out=rowsum[:, qb:qb + 1])
                if h is not None:
                    ex = nc.scalar.activation(esink[:], negmax[:], ACT.Exp, bias=sinkcol[:])
                ex.then_inc(p_done, 1)

            def gate(b, n):
                for t in range(2):
                    g = nc.scalar.activation(tile(gst, t), bank[b + t][:], ACT.Sigmoid)
                g.then_inc(act_evicted, 1)

            def high_output(dst, n):
                act.wait_ge(pv_done, n + 2)
                nc.scalar.activation(dst, bank[4][:], ACT.Copy).then_inc(o_hi_done, 1)

            def head_pair(h, last):
                for j in range(B_N):
                    split(ph_b, h, j, last)
                    if j == 1:
                        exponentials(fox_blocks, 2 * h + 1)
                    if j == 3:
                        act.wait_ge(p_turned, 2 * h + 1)
                        nc.scalar.activation(pt[:, 4 * P:7 * P], bank[5][:, 0:3 * P], ACT.Copy)
                        nc.scalar.activation(pt[:, 7 * P:10 * P], bank[6][:, 0:3 * P], ACT.Copy).then_inc(pt_act, 1)
                    if j == 4:
                        high_output(tile(of_hi, h), 2 * h + 1)
                        exponentials(swa_blocks, 2 * h + 2, h)
                        act.wait_ge(unit_done, B_R + B_N * h + 4)
                        gate(2, 0)
                    if j == 6:
                        act.wait_ge(p_turned, 2 * h + 2)
                        nc.scalar.activation(pt[:, 4 * P:7 * P], bank[6][:, 0:3 * P], ACT.Copy).then_inc(pt_act, 1)
                high_output(tile(oa_hi, h), 2 * h + 2)
                act.wait_ge(unit_done, B_R + B_N * h + 8)
                act.wait_ge(gate_spilled, 32 * h + 16)
                gate(0, 1)
            each(act, B_I, head_pair)

            def merge(i, last):
                for j in range(C_N):
                    split(ph_c, i, j, last)
                    if j == 3:
                        copy_cols(ADA_C + i)
                act.wait_ge(m_step, 6 * i + 12)
                for t in range(2):
                    nc.scalar.activation(tile(h_hi, 2 * i + t), tile(gates, t), ACT.Copy).then_inc(m_hi_done, 1)
            each(act, C_I, merge)

            def project(i, last):
                for j in range(D_N):
                    split(ph_d, i, j, last)
                    if j in (3, 7):
                        copy_cols(ADA_D + 2 * i + j // 4)
                    if j == 4:
                        squares(2 * i)
                squares(2 * i + 1)

            def squares(d):
                act.wait_ge(x2_done, 2 * d + 6)
                act.wait_ge(x2_summed, 2 * d + 2)
                for t in range(2):
                    nc.scalar.activation(tile(sq2, t), tile(x2, 2 * d + t), ACT.Square).then_inc(x2_squared, 1)
            each(act, D_I, project)
            act.wait_ge(r2_sum, 1)
            nc.scalar.activation(r2[:], bank[4][:], ACT.Sqrt, bias=eps[:], scale=1.0 / D).then_inc(r2_root, 1)
            for k in range(KD):
                act.wait_ge(h_full, KD + k + 1)
                nc.scalar.activation(tile(h_hi, k), tile(h2_full, k % 2), ACT.Copy).then_inc(h_hi_done, 1)
                if k in UNITS_BETWEEN:
                    split(ph_e, 0, UNITS_BETWEEN.index(k), False)

            def ffn(i, last, first=False):
                for j in range(E_N):
                    if not (first and j < len(UNITS_BETWEEN)):
                        split(ph_e, i, j, last)
                    if j in (4, 12):
                        act.wait_ge(unit_done, E_R + E_N * i + j)
                        if j == 12:
                            act.wait_ge(u_mul, 4 * i + 2)
                        for t in range(2):
                            g = nc.scalar.activation(tile(sg, t), bank[2 + t][:], ACT.Silu)
                        g.then_inc(act_evicted, 1)
                    if j in (8, 16):
                        for t in range(2):
                            n = (j - 8) // 4 + t
                            act.wait_ge(u_mul, 4 * i + n + 1)
                            nc.scalar.activation(tile(u_hi, n), tile(u_full, t), ACT.Copy).then_inc(u_hi_done, 1)
            ffn(0, False, True)
            each(act, E_I, ffn, 1)

            for m in range(TB * TB):
                if m % 2 == 0:
                    act.wait_ge(o_block_turned, m + 1)
                    tb, n4 = m % TB, m // TB
                    nc.scalar.activation(out_rows[:, tb * D + n4 * S:tb * D + (n4 + 1) * S], bank[(m + 4) % 8][:],
                                         ACT.Copy).then_inc(out_copied_a, 1)

        @block.vector
        def _(dve):
            v = nc.vector

            def split(ph, i, j, last):
                at_ = ahead(ph, i, j, last)
                if at_ is None:
                    return
                r, slot, use = numbers(*at_)
                dve.wait_ge(hi_done, r + 1)
                ws = numbers(at_[0], 0, at_[2])[0] % RING
                n = P if at_[0] is ph_f else UN
                raw, hi, lo = [unit(t, s).rearrange("p (k n) -> p k n", k=UK)[:, :, 0:n]
                               for t, s in ((w_raw, slot), (w_hi, ws), (w_lo, ws))]
                v.tensor_tensor(lo, raw, hi.bitcast(F32), ALU.subtract).then_inc(lo_done, 1)
                p, ii, jj = at_
                if p["ada"] is not None:
                    acc = ada_acc if p is ph_a else ada_acc2
                    mac(p["ada"] + p["n"] // STEP * ii + jj // STEP, jj % STEP, p["u"] + 2 * jj + 1,
                        ii * (2 * p["n"] // RING), acc, jj // STEP % 2, p is not ph_a)

            def mac(s, kq, u, uses, accs, s_set, strict):
                if u is None:
                    dve.wait_ge(shift_landed[kq], 16 * uses + 16)
                    w = shift_raw[kq]
                else:
                    dve.wait_ge(raw_landed[u % RING], (u // RING + uses) * 32 + 32)
                    w = unit(w_raw, u)
                for k in range(UK):
                    acc = accs[:, (2 * s_set + k % 2) * UN:(2 * s_set + k % 2 + 1) * UN]
                    wk, ck = w[:, k * UN:(k + 1) * UN], cact[:, kq * UK + k:kq * UK + k + 1]
                    if kq == 0 and k < 2:
                        if k == 0:
                            dve.wait_ge(ada_summed, s + (2 if strict else 1))
                        v.tensor_scalar(acc, wk, ck, None, ALU.mult).then_inc(ada_mac, 1)
                    else:
                        dve.wait_ge(ada_mac, s * STEP * UK + kq * UK + k - 1)
                        v.scalar_tensor_tensor(out=acc, in0=wk, scalar=ck, in1=acc, op0=ALU.mult,
                                               op1=ALU.add).then_inc(ada_mac, 1)

            v.memset(vecrows[:], 0.0).then_inc(vec_zeroed, 1)
            v.memset(eps[:], EPS)
            v.memset(ones[:], 1.0).then_inc(ones_set, 1)
            v.memset(fq_rows[:].bitcast(F32), 0.0)
            v.memset(fk_rows[:].bitcast(F32), 0.0).then_inc(rows_zeroed, 1)
            dve.wait_ge(rows_zeroed, 1)
            for r0 in (64, 96):
                v.memset(fq_rows[r0:r0 + HQ, :].bitcast(F32), 1.0)
            v.memset(fk_rows[32:32 + HQ, :].bitcast(F32), 1.0).then_inc(f_dve, 1)
            dve.wait_ge(vecs_turned, 1)
            v.tensor_copy(vec[:], bank[5][:, 0:64]).then_inc(vecs_copied, 1)
            v.tensor_copy(bada[:], bank[5][:, P:P + 6 * KD]).then_inc(vecs_copied, 1)
            dve.wait_ge(vecs_copied, 2)
            n0 = 3 * KD
            v.tensor_copy(wy[:, 0:1], vec[:, n0 + 1:n0 + 2])
            v.tensor_scalar(wy[:, 1:2], vec[:, n0:n0 + 1], SCALE, None, ALU.mult)
            v.tensor_scalar(wx[:, 0:1], vec[:, n0 + 2:n0 + 3], SCALE, None, ALU.mult)
            v.tensor_copy(wx[:, 1:2], vec[:, n0 + 3:n0 + 4]).then_inc(weights_ready, 1)
            dve.wait_ge(cact_done, 1)
            def scale_step(p):
                for kq in range(STEP):
                    mac(2 * p, kq, kq, p, ada_acc, 0, False)

            def shift_step(p):
                for kq in range(STEP):
                    mac(2 * p + 1, kq, None, p, ada_acc, 1, False)

            scale_step(0)
            dve.wait_ge(r_root, 1)
            v.reciprocal(rr[:], rr[:]).then_inc(r_ready, 1)
            dve.wait_ge(r_ready, 1)
            for tb in range(TB):
                v.tensor_scalar(diag[:, tb * P:(tb + 1) * P], ident[:], rr[:, tb:tb + 1], None,
                                ALU.mult).then_inc(diag_ready, 1)
            shift_step(0)
            with dve.Fori(1, G_N) as p:
                scale_step(p)
                shift_step(p)

            for j in range(LEAD):
                split(ph_f, 0, j - LEAD, False)

            def y_norm(y):
                dve.wait_ge(y_rooted, y + 1)
                v.reciprocal(tile(rs, 0), tile(rs, 0)).then_inc(y_chain, 1)

            for j in range(4):
                split(ph_f, 0, j, True)
                if j == 2:
                    y_norm(0)
            f0, z = fz[0:HQ, 0:S], fz[0:HQ, S:2 * S]

            def forget():
                dve.wait_ge(f_act, 2)
                v.scalar_tensor_tensor(out=z, in0=z, scalar=0.0, in1=f0, op0=ALU.min,
                                       op1=ALU.subtract).then_inc(f_dve, 1)
                dve.wait_ge(f_dve, 3)
                v.tensor_tensor_scan(f0, z, z, 0.0, ALU.add, ALU.min).then_inc(f_dve, 1)
                dve.wait_ge(f_dve, 4)
                v.tensor_copy(fk_rows[0:HQ, :], f0).then_inc(f_dve, 1)
                dve.wait_ge(f_dve, 5)
                hi = fk_rows[0:HQ, :].bitcast(F32)
                v.tensor_tensor(fq_rows[32:32 + HQ, :], f0, hi, ALU.subtract)
                v.tensor_scalar(fk_rows[64:64 + HQ, :], hi, -1.0, None, ALU.mult).then_inc(f_dve, 1)
                dve.wait_ge(f_dve, 6)
                v.tensor_scalar(fk_rows[96:96 + HQ, :], fq_rows[32:32 + HQ, :].bitcast(F32), -1.0, None, ALU.mult)
                v.tensor_copy(fq_rows[0:HQ, :], hi).then_inc(f_dve, 1)
                dve.wait_ge(f_dve, 7)
                v.memset(fk_rows[0:HQ, :].bitcast(F32), 1.0).then_inc(f_dve, 1)

            def heads(i, last):
                for j in range(A_N):
                    split(ph_a, i, j, last)
                    if j == 1:
                        y_norm(i + 1)
                    if j == 2 and last:
                        dve.wait_ge(act_evicted, 3)
                        v.scalar_tensor_tensor(out=f0, in0=z, scalar=-1.0, in1=z, op0=ALU.mult,
                                               op1=ALU.min).then_inc(f_dve, 1)
                    if j == 4 and last:
                        forget()
                    if j == 5:
                        for t in range(2):
                            dve.wait_ge((x_rooted, x_stats)[t], i + 1)
                            v.reciprocal(tile(rs, t), tile(rs, t)).then_inc(x_chain, 1)
            each(dve, A_I, heads)
            y_norm(KVH + HQ - 1)

            def forget_rows(h):
                v.tensor_scalar(fq_head[:], fq_rows[:].bitcast(F32), col(sel, h), None, ALU.mult).then_inc(fq_done, 1)

            dve.wait_ge(f_dve, 8)
            forget_rows(0)
            y_rotate(dve, KVH + HQ - 1)

            def masked(blocks, where, mask, n, stats, h=None):
                dve.wait_ge(masks_landed, 32)
                if h is not None:
                    dve.wait_ge(sink_set, h + 1)
                dve.wait_ge(s_done, n)
                v.memset(negmax[:], 0.0)
                for qb, b0 in enumerate(starts(blocks)):
                    bk, c0 = where[qb]
                    w = len(blocks[qb]) * P
                    wide = mask.shape[1]
                    v.tensor_tensor_reduce(out=logits[:, b0 * P:b0 * P + w], in0=bank[bk][:, c0:c0 + w],
                                           in1=mask[:, wide - w:wide], scale=1.0, scalar=-3.0e38, op0=ALU.add,
                                           op1=ALU.max, accum_out=rowmax[:, qb:qb + 1]).then_inc(s_stats, 1)
                dve.wait_ge(s_stats, stats)
                if h is None:
                    v.tensor_scalar(negmax[:], rowmax[:], -1.0, None, ALU.mult).then_inc(negmax_done, 1)
                else:
                    v.tensor_scalar(negmax[:], rowmax[:], sinkcol[:], -1.0, ALU.max, ALU.mult).then_inc(negmax_done, 1)

            def normalise(blocks, n, h=None):
                dve.wait_ge(p_done, n)
                if h is not None:
                    v.tensor_tensor(rowsum[:], rowsum[:], esink[:], ALU.add).then_inc(sums_added, 1)
                    dve.wait_ge(sums_added, h + 1)
                v.reciprocal(rinv[:], rowsum[:]).then_inc(rinv_done, 1)
                dve.wait_ge(rinv_done, n)
                for qb, b0 in enumerate(starts(blocks)):
                    w = slice(b0 * P, (b0 + len(blocks[qb])) * P)
                    ins = v.tensor_scalar(logits[:, w], logits[:, w], rinv[:, qb:qb + 1], None, ALU.mult)
                ins.then_inc(p_scaled, 1)

            def low_output(dst, hi, n):
                dve.wait_ge(o_hi_done, n)
                v.tensor_tensor(dst, bank[4][:], hi.bitcast(F32), ALU.subtract).then_inc(o_ready, 1)


            def head_pair(h, last):
                v.tensor_copy(sinkcol[:], col(sinks, h)).then_inc(sink_set, 1)
                for j in range(B_N):
                    split(ph_b, h, j, last)
                    if j == 1:
                        masked(fox_blocks, fox_at, foxmask, 2 * h + 1, 8 * h + 4)
                    if j == 2:
                        normalise(fox_blocks, 2 * h + 1)
                    if j == 3:
                        dve.wait_ge(p_turned, 2 * h + 1)
                        v.tensor_copy(pt[:, 0:4 * P], bank[7][:]).then_inc(pt_dve, 1)
                    if j == 4:
                        masked(swa_blocks, swa_at, swamask, 2 * h + 2, 8 * h + 8, h)
                    if j == 5:
                        low_output(tile(of_lo, h), tile(of_hi, h), 2 * h + 1)
                        normalise(swa_blocks, 2 * h + 2, h)
                    if j == 6:
                        dve.wait_ge(p_turned, 2 * h + 2)
                        v.tensor_copy(pt[:, 0:4 * P], bank[7][:]).then_inc(pt_dve, 1)
                low_output(tile(oa_lo, h), tile(oa_hi, h), 2 * h + 2)
                if not last:
                    dve.wait_ge(pv_done, 2 * h + 4)
                    forget_rows(h + 1)
            each(dve, B_I, head_pair)

            def merge(i, last):
                def gated(t4, b):
                    v.tensor_tensor(tile(gates, t4), bank[b][:], tile(gates, t4), ALU.mult).then_inc(m_step, 1)

                for j in range(C_N):
                    split(ph_c, i, j, last)
                    if j == 2:
                        dve.wait_ge(unit_done, C_R + C_N * i + 2)
                        dve.wait_ge(gates_landed, 32 * i + 32)
                        gated(0, 2)
                        gated(1, 3)
                dve.wait_ge(unit_done, C_R + C_N * i + 4)
                gated(2, 0)
                gated(3, 1)
                dve.wait_ge(m_step, 6 * i + 10)
                for t in range(2):
                    v.tensor_tensor(tile(gates, t), tile(gates, t), tile(gates, 2 + t), ALU.add).then_inc(m_step, 1)
                for t in range(2):
                    dve.wait_ge(m_hi_done, 2 * i + t + 1)
                    v.tensor_tensor(tile(h_lo, 2 * i + t), tile(gates, t), tile(h_hi, 2 * i + t).bitcast(F32),
                                    ALU.subtract).then_inc(m_ready, 1)
            each(dve, C_I, merge)

            def residual(i, q):
                d = 2 * i + q
                dve.wait_ge(unit_done, D_R + D_N * i + 4 * q + 4)
                dve.wait_ge(xr_landed[q], 16 * i + 16)
                for t in range(2):
                    v.scalar_tensor_tensor(out=tile(x2, 2 * d + t), in0=bank[(2, 0)[q] + t][:],
                                           scalar=col(mod, 2 * KD + 2 * d + t), in1=tile(xr, 2 * q + t),
                                           op0=ALU.mult, op1=ALU.add).then_inc(x2_done, 1)

            def project(i, last):
                for j in range(D_N):
                    split(ph_d, i, j, last)
                    if j == 4:
                        residual(i, 0)
                residual(i, 1)
            dve.wait_ge(mod_ready, ADA_C + 1)
            each(dve, D_I, project)
            dve.wait_ge(mod_ready, 3 * KD + 1)
            v.scalar_tensor_tensor(out=a2[:], in0=mod[:, 4 * KD:5 * KD], scalar=1.0, in1=vec[:, 2 * KD:3 * KD],
                                   op0=ALU.add, op1=ALU.mult)
            dve.wait_ge(r2_root, 1)
            v.reciprocal(r2[:], r2[:]).then_inc(r2_ready, 1)
            dve.wait_ge(r2_ready, 1)
            for k in range(KD):
                v.tensor_tensor(tile(h2_t, k % 2), tile(x2, k), r2[:], ALU.mult).then_inc(h2_scaled, 1)
                dve.wait_ge(h2_scaled, k + 1)
                dve.wait_ge(h_ready, KD + k + 1)
                v.tensor_scalar(tile(h2_full, k % 2), tile(h2_t, k % 2), a2[:, k:k + 1],
                                mod[:, 3 * KD + k:3 * KD + k + 1], ALU.mult, ALU.add).then_inc(h_full, 1)
                if k - 1 in UNITS_BETWEEN:
                    split(ph_e, 0, UNITS_BETWEEN.index(k - 1), False)

            def ffn(i, last, first=False):
                for j in range(E_N):
                    if not (first and j < len(UNITS_BETWEEN)):
                        split(ph_e, i, j, last)
                    if j in (8, 16):
                        dve.wait_ge(unit_done, E_R + E_N * i + j)
                        dve.wait_ge(act_evicted, 2 * i + 36 + (j - 8) // 8)
                        for t in range(2):
                            v.tensor_tensor(tile(u_full, t), bank[t][:], tile(sg, t), ALU.mult).then_inc(u_mul, 1)
                        for t in range(2):
                            n = (j - 8) // 4 + t
                            dve.wait_ge(u_hi_done, 4 * i + n + 1)
                            v.tensor_tensor(tile(u_lo, n), tile(u_full, t), tile(u_hi, n).bitcast(F32),
                                            ALU.subtract).then_inc(u_ready, 1)
                    if j > 16:
                        accumulate(i, j - 17)
                accumulate(i, 7)

            def accumulate(i, q):
                dve.wait_ge(unit_done, E_R + E_N * i + 17 + q)
                for t in range(2):
                    n = 2 * q + t
                    ins = v.scalar_tensor_tensor(out=tile(x2, n), in0=bank[(4, 6, 2, 0)[q % 4] + t][:],
                                                 scalar=mod[:, 5 * KD + n:5 * KD + n + 1], in1=tile(x2, n),
                                                 op0=ALU.mult, op1=ALU.add)
                ins.then_inc(acc_done, 1)
            ffn(0, False, True)
            each(dve, E_I, ffn, 1)

            for m in range(TB * TB):
                if m % 2 == 1:
                    dve.wait_ge(o_block_turned, m + 1)
                    tb, n4 = m % TB, m // TB
                    v.tensor_copy(out_rows[:, tb * D + n4 * S:tb * D + (n4 + 1) * S],
                                  bank[(m + 4) % 8][:]).then_inc(out_copied_d, 1)

        @block.gpsimd
        def _(pool):
            g = nc.gpsimd
            pool.sem_inc(ada_summed, 2)
            for s in (ada_cols, col_copied, mod_ready, y_stats):
                pool.sem_inc(s, 1)
            for s in (h_ready, pv_done, o_ready, m_ready, x2_summed):
                pool.sem_inc(s, 2)
            pool.sem_inc(x_chain, 4)
            pool.sem_inc(x2_done, 4)
            pool.sem_inc(m_step, 6)
            pool.sem_inc(acc_done, 8)

            def add_halves(s, accs, s_set):
                pool.wait_ge(ada_mac, s * (STEP * UK) + STEP * UK)
                pool.wait_ge(ada_cols, s + 1)
                even, odd = (accs[:, (2 * s_set + n) * UN:(2 * s_set + n + 1) * UN] for n in range(2))
                g.tensor_tensor(ada_sum[:], even, odd, ALU.add).then_inc(ada_summed, 1)

            def add_bias(s, ct):
                pool.wait_ge(col_copied, s + 2)
                g.tensor_tensor(col(mod, ct, 2), colraw[:], col(bada, ct, 2), ALU.add).then_inc(mod_ready, 1)

            def step(s, accs, s_set, ct):
                add_halves(s, accs, s_set)
                add_bias(s, ct)

            add_halves(0, ada_acc, 0)

            def low(k, t, kk, fl):
                pool.wait_ge(h_hi_done, k + 1)
                g.tensor_tensor(tile(h_lo, kk), tile(fl, t), tile(h_hi, kk).bitcast(F32),
                                ALU.subtract).then_inc(h_ready, 1)

            def pair(i, q, last):
                add_bias(2 * i, 2 * i + KD)
                pool.wait_ge(mod_ready, 2 * i + 2)
                g.tensor_tensor(col(a1, 2 * i, 2), col(mod, 2 * i + KD, 2), ones[:, 0:2], ALU.add).then_inc(a1_step, 1)
                pool.wait_ge(a1_step, i + 1)
                g.tensor_tensor(col(a1, 2 * i, 2), col(a1, 2 * i, 2), col(vec, 2 * i + KD, 2),
                                ALU.mult).then_inc(scale_ready, 1)
                step(2 * i + 1, ada_acc, 1, 2 * i)
                pool.wait_ge(hi_done, i + 1)
                g.tensor_tensor(unit(w_lo, q % 2), g_raw[:, (q % 2) * UK * UN:(q % 2 + 1) * UK * UN],
                                unit(w_hi, q % 2).bitcast(F32), ALU.subtract).then_inc(lo_done, 1)
                for t in range(2):
                    low(2 * i + t, t, 2 * i + t, full)
                if not last:
                    add_halves(2 * i + 2, ada_acc, 0)

            def pairs(i, last):
                for q in range(2):
                    pair(2 * i + q, q, last and q == 1)
            each(pool, G_N // 2, pairs)

            pool.wait_ge(tab_landed, 16 * 5)
            y_rotate(pool, 0)
            with pool.Fori(0, A_I) as i:
                s = ADA_A + 2 * i
                add_halves(s, ada_acc, 0)
                y_rotate(pool, i + 1)
                add_bias(s, 2 * ADA_A + 4 * i)
                add_halves(s + 1, ada_acc, 1)
                pool.wait_ge(x_chain, 4 * i + 6)
                for t, hd in enumerate((qf, kf)):
                    g.tensor_tensor(tile(hd, i), tile(hd, i), tile(rs, t), ALU.mult).then_inc(x_chain, 1)
                add_bias(s + 1, 2 * ADA_A + 4 * i + 2)
            pool.wait_ge(y_posts, KVH + HQ)
            pool.wait_ge(x_chain, 4 * HQ + 4)
            g.tensor_copy(q_fox[:], tile(qf, 0)).then_inc(q_copied, 1)
            pool.wait_ge(y_chain, 6 * (KVH + HQ))
            c0 = P + 2 * S
            pool.dma_start(foxmask[:], consts[:, c0:c0 + S]).then_inc(masks_landed, 16)
            pool.dma_start(swamask[:], consts[:, c0 + S:c0 + S + 2 * P]).then_inc(masks_landed, 16)
            g.tensor_copy(q_swa[:], tile(rot, KVH)).then_inc(q_copied, 1)

            def spills(h, last):
                for q in range(2):
                    pool.wait_ge(p_turned, 2 * h + 1 + q)
                    g.tensor_copy(v_head[:], val[:, bass.ds(((h // GROUP) if q else (h + KVH)) * S, S)]
                                  ).then_inc(v_copied, 1)
                    pool.wait_ge(act_evicted, 2 * h + 20 + q)
                    pool.dma_start(gate_fm[bass.ds(2 * h + q * KD, 2)].rearrange("k p s -> p k s"),
                                   gst[:].rearrange("p (k s) -> p k s", k=2)).then_inc(gate_spilled, 16)
                if not last:
                    pool.wait_ge(pv_done, 2 * h + 4)
                    g.tensor_copy(q_fox[:], tile(qf, h + 1)).then_inc(q_copied, 1)
                    pool.wait_ge(gate_spilled, 32 * h + 32)
                    g.tensor_copy(q_swa[:], tile(rot, h + 1 + KVH)).then_inc(q_copied, 1)
            each(pool, B_I, spills)

            pool.wait_ge(gate_spilled, 32 * B_I)
            with pool.Fori(0, C_I) as i:
                pool.wait_ge(m_ready, 2 * i + 2)
                for q in range(2):
                    pool.dma_start(gates[:, 2 * q * S:(2 * q + 2) * S].rearrange("p (k s) -> p k s", k=2),
                                   gate_fm[bass.ds(2 * i + q * KD, 2)].rearrange("k p s -> p k s")
                                   ).then_inc(gates_landed, 16)
                step(ADA_C + i, ada_acc2, 0, 2 * ADA_C + 2 * i)

            pool.wait_ge(unit_done, D_R)
            g.memset(sumsq[:], 0.0).then_inc(sumsq_zero, 1)
            pool.wait_ge(sumsq_zero, 1)

            def add_squares(d):
                for t in range(2):
                    pool.wait_ge(x2_squared, 2 * d + t + 1)
                    pool.wait_ge(x2_summed, 2 * d + t + 2)
                    g.tensor_tensor(sumsq[:], sumsq[:], tile(sq2, t), ALU.add).then_inc(x2_summed, 1)

            pool.wait_ge(x_spilled, 16 * 4)

            def residuals(i, last):
                for q in range(2):
                    pool.wait_ge(x2_done, 4 * i + 2 * q + 2)
                    pool.dma_start(xr[:, 2 * q * S:(2 * q + 2) * S].rearrange("p (k s) -> p k s", k=2),
                                   x_fm[bass.ds(4 * i + 2 * q, 2)].rearrange("k p s -> p k s")
                                   ).then_inc(xr_landed[q], 16)
                for q in range(2):
                    step(ADA_D + 2 * i + q, ada_acc2, q, 2 * ADA_D + 4 * i + 2 * q)
                    if not (last and q == 1):
                        add_squares(2 * i + q)
            each(pool, D_I, residuals)

            for k in range(KD):
                low(KD + k, k % 2, k, h2_full)


_INS = ["x", "c", "w_ada", "b_ada", "norm1_w", "w_in", "b_forget", "swa_q_norm_w", "swa_k_norm_w",
        "swa_sinks", "fox_q_norm_w", "fox_k_norm_w", "w_o_swa", "w_o_fox", "w_out", "norm2_w",
        "w_ffn_in", "w_ffn_out"]


def kernel(**inputs):
    import concourse.bacc as bacc
    from concourse.bass_utils import run_bass_kernel_spmd

    nc = bacc.Bacc("TRN2", target_bir_lowering=False, num_devices=1)
    arrays, args = {}, []
    for name in _INS:
        a = np.ascontiguousarray(inputs[name])
        arrays[f"in_{name}"] = a
        args.append(nc.dram_tensor(f"in_{name}", a.shape, mybir.dt.from_np(a.dtype), kind="ExternalInput").ap())
    table = shape_constants()
    arrays["in_consts"] = table
    args.append(nc.dram_tensor("in_consts", table.shape, F32, kind="ExternalInput").ap())
    args.append(nc.dram_tensor("out", (1, S, D), F32, kind="ExternalOutput").ap())
    build_block(nc, *args)
    result = run_bass_kernel_spmd(nc, [arrays], core_ids=[0])
    return result.results[0]["out"]
```
